# Optimizing a Trainium2 kernel written in Bass

```python
import jax, jax.numpy as jnp
from jax import lax
import numpy as np

D_MODEL = 2048
BATCH = 1
SEQ = 256
DEPTH = 1

CHUNK = 64
EPS = 1e-6
M_HEADS = 4
M_DV = 256
M_DQK = 128
M_WIDTH = M_HEADS * M_DV
M_QK_WIDTH = M_HEADS * M_DQK
C_WIDTH = 1024
C_GROUPS = 8
C_KERNEL = 3
D_FF = 5504
F_KERNEL = 3
SPLIT_SIZES = (M_QK_WIDTH, M_QK_WIDTH, M_WIDTH, M_WIDTH, M_HEADS, M_HEADS,
               C_WIDTH, C_WIDTH, C_WIDTH, D_MODEL, D_MODEL)
IN_WIDTH = sum(SPLIT_SIZES)
F_GATE_OFFSET = 2 * M_QK_WIDTH + 2 * M_WIDTH + M_HEADS


def rmsnorm(x, g):
    x32 = x.astype(jnp.float32)
    y = x32 * lax.rsqrt(jnp.mean(x32 * x32, axis=-1, keepdims=True) + EPS)
    return (y * g.astype(jnp.float32)).astype(x.dtype)

def causal_dwconv(x, w, b=None):
    K = w.shape[0]
    T = x.shape[1]
    xp = jnp.pad(x, ((0, 0), (K - 1, 0), (0, 0)))
    y = xp[:, 0:T, :] * w[0]
    for j in range(1, K):
        y = y + xp[:, j:j + T, :] * w[j]
    if b is not None:
        y = y + b
    return y

def mlstm_chunkwise(q, k, v, i_pre, f_pre):
    B, T, H, DQK = q.shape
    DV = v.shape[-1]
    NC = T // CHUNK
    L = CHUNK
    f32 = jnp.float32

    def to_chunks(a):
        a = jnp.moveaxis(a.astype(f32), 2, 1)
        return a.reshape((B, H, NC, L) + a.shape[3:])

    qc = to_chunks(q)
    kc = to_chunks(k) * (DQK ** -0.5)
    vc = to_chunks(v)
    logi = to_chunks(i_pre)
    logf = jax.nn.log_sigmoid(to_chunks(f_pre))

    b = jnp.cumsum(logf, axis=-1)
    a = b[..., -1]
    w = a[..., None] - b + logi
    m_loc = jnp.max(w, axis=-1)
    p = jnp.exp(w - m_loc[..., None])
    C_loc = jnp.einsum('bhcs,bhcsv,bhcsk->bhcvk', p, vc, kc)
    n_loc = jnp.einsum('bhcs,bhcsk->bhck', p, kc)

    def step(carry, xs):
        C, n, m = carry
        a_c, ml, Cl, nl = xs
        m_new = jnp.maximum(a_c + m, ml)
        s_old = jnp.exp(a_c + m - m_new)
        s_new = jnp.exp(ml - m_new)
        C_new = s_old[..., None, None] * C + s_new[..., None, None] * Cl
        n_new = s_old[..., None] * n + s_new[..., None] * nl
        return (C_new, n_new, m_new), (C, n, m)

    init = (jnp.zeros((B, H, DV, DQK), f32), jnp.zeros((B, H, DQK), f32), jnp.zeros((B, H), f32))
    xs = (jnp.moveaxis(a, 2, 0), jnp.moveaxis(m_loc, 2, 0),
          jnp.moveaxis(C_loc, 2, 0), jnp.moveaxis(n_loc, 2, 0))
    _, (C_prev, n_prev, m_prev) = lax.scan(step, init, xs)
    C_prev = jnp.moveaxis(C_prev, 0, 2)
    n_prev = jnp.moveaxis(n_prev, 0, 2)
    m_prev = jnp.moveaxis(m_prev, 0, 2)

    causal = jnp.tril(jnp.ones((L, L), dtype=bool))
    Dm = b[..., :, None] - b[..., None, :] + logi[..., None, :]
    Dm = jnp.where(causal, Dm, -jnp.inf)
    m_inter = b + m_prev[..., None]
    m_t = jnp.maximum(jnp.max(Dm, axis=-1), m_inter)
    S = jnp.einsum('bhctk,bhcsk->bhcts', qc, kc) * jnp.exp(Dm - m_t[..., None])
    inter_scale = jnp.exp(m_inter - m_t)
    num = (jnp.einsum('bhcts,bhcsv->bhctv', S, vc)
           + inter_scale[..., None] * jnp.einsum('bhcvk,bhctk->bhctv', C_prev, qc))
    den = jnp.sum(S, axis=-1) + inter_scale * jnp.einsum('bhck,bhctk->bhct', n_prev, qc)
    h = num / jnp.maximum(jnp.abs(den), jnp.exp(-m_t))[..., None]
    h = h.reshape(B, H, T, DV)
    return jnp.moveaxis(h, 1, 2)

def first_inputs(seed: int = 0) -> dict:
    key = jax.random.key(seed)
    ks = jax.random.split(key, 16)
    f32 = jnp.float32
    nrm = lambda k, shape, scale: (jax.random.normal(k, shape, f32) * scale)
    x = jax.random.normal(ks[0], (BATCH, SEQ, D_MODEL), f32)
    norm_mix_g = 1.0 + nrm(ks[1], (D_MODEL,), 0.02)
    w_in = nrm(ks[2], (D_MODEL, IN_WIDTH), D_MODEL ** -0.5)
    b_in = nrm(ks[3], (IN_WIDTH,), 0.02)
    b_in = b_in.at[F_GATE_OFFSET:F_GATE_OFFSET + M_HEADS].add(jnp.linspace(3.0, 6.0, M_HEADS))
    mlstm_head_g = 1.0 + nrm(ks[4], (M_WIDTH,), 0.02)
    w_branch_m = nrm(ks[5], (M_WIDTH, D_MODEL), M_WIDTH ** -0.5)
    conv_w = nrm(ks[6], (C_KERNEL, C_WIDTH), C_KERNEL ** -0.5)
    w_branch_c = nrm(ks[7], (C_WIDTH, D_MODEL), C_WIDTH ** -0.5)
    w_out = nrm(ks[8], (D_MODEL, D_MODEL), D_MODEL ** -0.5)
    norm_ffn_g = 1.0 + nrm(ks[9], (D_MODEL,), 0.02)
    w_up = nrm(ks[10], (D_MODEL, 2 * D_FF), D_MODEL ** -0.5)
    ffn_conv_w = nrm(ks[11], (F_KERNEL, 2 * D_FF), F_KERNEL ** -0.5)
    ffn_conv_b = nrm(ks[12], (2 * D_FF,), 0.02)
    w_down = nrm(ks[13], (D_FF, D_MODEL), D_FF ** -0.5)
    norm_out_g = 1.0 + nrm(ks[14], (D_MODEL,), 0.02)
    return {"x": x, "norm_mix_g": norm_mix_g, "w_in": w_in, "b_in": b_in,
            "mlstm_head_g": mlstm_head_g, "w_branch_m": w_branch_m, "conv_w": conv_w,
            "w_branch_c": w_branch_c, "w_out": w_out, "norm_ffn_g": norm_ffn_g,
            "w_up": w_up, "ffn_conv_w": ffn_conv_w, "ffn_conv_b": ffn_conv_b,
            "w_down": w_down, "norm_out_g": norm_out_g}

def first_block(x, norm_mix_g, w_in, b_in, mlstm_head_g, w_branch_m, conv_w, w_branch_c,
              w_out, norm_ffn_g, w_up, ffn_conv_w, ffn_conv_b, w_down, norm_out_g):
    B, T, _ = x.shape
    h = x
    for _layer in range(DEPTH):
        hn = rmsnorm(h, norm_mix_g)
        proj = hn @ w_in + b_in
        offs = [int(o) for o in np.cumsum(SPLIT_SIZES)[:-1]]
        (q, k, v, o_pre, i_pre, f_pre, cb, cc, ch, gm_pre, gc_pre) = jnp.split(proj, offs, axis=-1)

        hm = mlstm_chunkwise(q.reshape(B, T, M_HEADS, M_DQK), k.reshape(B, T, M_HEADS, M_DQK),
                             v.reshape(B, T, M_HEADS, M_DV), i_pre, f_pre)
        hm = hm * lax.rsqrt(jnp.mean(hm * hm, axis=-1, keepdims=True) + EPS)
        hm = hm.reshape(B, T, M_WIDTH) * mlstm_head_g.astype(jnp.float32)
        hm = hm.astype(x.dtype) * jax.nn.sigmoid(o_pre)
        y_m = hm @ w_branch_m

        y_c = (cb * causal_dwconv(cc * ch, conv_w)) @ w_branch_c

        merged = jax.nn.sigmoid(gm_pre) * y_m + jax.nn.sigmoid(gc_pre) * y_c
        h = h + merged @ w_out

        hn = rmsnorm(h, norm_ffn_g)
        u = causal_dwconv(hn @ w_up, ffn_conv_w, ffn_conv_b)
        gate, val = jnp.split(u, 2, axis=-1)
        h = h + (jax.nn.silu(gate) * val) @ w_down
    return rmsnorm(h, norm_out_g)


N_META = 16
POOL_WIDTH = D_MODEL
POOL_WINDOWS = (2, 4, 8, 16)
POOL_GROUPS = len(POOL_WINDOWS)
POOL_GROUP_DIM = POOL_WIDTH // POOL_GROUPS
LRU_WIDTH = D_MODEL
LRU_HEAD_DIM = 256
LRU_HEADS = LRU_WIDTH // LRU_HEAD_DIM
CONV_WIDTH = 4
LRU_C = 8.0
D_FF_2 = 4 * D_MODEL
NORM_EPS = 1e-6
IN_SPLITS = (POOL_WIDTH,
             POOL_WIDTH + LRU_WIDTH,
             POOL_WIDTH + 2 * LRU_WIDTH,
             POOL_WIDTH + 2 * LRU_WIDTH + D_MODEL)
IN_COLS = POOL_WIDTH + 2 * LRU_WIDTH + 2 * D_MODEL


def rmsnorm_2(x, g):
    xf = x.astype(jnp.float32)
    y = xf * lax.rsqrt(jnp.mean(xf * xf, axis=-1, keepdims=True) + NORM_EPS)
    return (y * g.astype(jnp.float32)).astype(x.dtype)

def causal_window_mean(v, w):
    T = v.shape[1]
    c = lax.cumsum(v, axis=1)
    c_shift = jnp.pad(c, ((0, 0), (w, 0), (0, 0)))[:, :T]
    cnt = jnp.minimum(jnp.arange(1, T + 1), w).astype(jnp.float32)
    return (c - c_shift) / cnt[None, :, None]

def pool_mixer(v, pool_w, pool_scale):
    B, T, _ = v.shape
    vf = v.astype(jnp.float32)
    diffs = []
    for g, w in enumerate(POOL_WINDOWS):
        vg = vf[..., g * POOL_GROUP_DIM:(g + 1) * POOL_GROUP_DIM]
        diffs.append(causal_window_mean(vg, w) - vg)
    d = jnp.stack(diffs, axis=2)
    y = jnp.einsum('btgc,gcd->btgd', d, pool_w.astype(jnp.float32))
    y = y.reshape(B, T, POOL_WIDTH) * pool_scale.astype(jnp.float32)
    return y.astype(v.dtype)

def causal_depthwise_conv(x, w, b):
    y = lax.conv_general_dilated(
        x, w[:, None, :].astype(x.dtype), window_strides=(1,),
        padding=((CONV_WIDTH - 1, 0),),
        dimension_numbers=('NWC', 'WIO', 'NWC'),
        feature_group_count=x.shape[-1])
    return y + b.astype(x.dtype)

def rg_lru(xc, gate_a_w, gate_a_b, gate_x_w, gate_x_b, lam):
    B, T, W = xc.shape
    xf = xc.astype(jnp.float32)
    xh = xf.reshape(B, T, LRU_HEADS, LRU_HEAD_DIM)
    r = jax.nn.sigmoid(jnp.einsum('bthi,hij->bthj', xh, gate_a_w.astype(jnp.float32))
                       + gate_a_b.astype(jnp.float32)).reshape(B, T, W)
    i = jax.nn.sigmoid(jnp.einsum('bthi,hij->bthj', xh, gate_x_w.astype(jnp.float32))
                       + gate_x_b.astype(jnp.float32)).reshape(B, T, W)
    log_a = -LRU_C * r * jax.nn.softplus(-lam.astype(jnp.float32))
    a = jnp.exp(log_a)
    mult = jnp.sqrt(-jnp.expm1(2.0 * log_a))
    bt = mult * (i * xf)

    def combine(left, right):
        a1, b1 = left
        a2, b2 = right
        return a1 * a2, a2 * b1 + b2

    _, h = lax.associative_scan(combine, (a, bt), axis=1)
    return h.astype(xc.dtype)

def second_inputs(seed: int = 0) -> dict:
    key = jax.random.key(seed)
    ks = jax.random.split(key, 20)
    f32 = jnp.float32
    x = jax.random.normal(ks[0], (BATCH, SEQ, D_MODEL), f32)
    meta_tokens = jax.random.normal(ks[1], (N_META, D_MODEL), f32)
    norm1_g = 1.0 + 0.02 * jax.random.normal(ks[2], (DEPTH, D_MODEL), f32)
    w_in = jax.random.normal(ks[3], (DEPTH, D_MODEL, IN_COLS), f32) * D_MODEL ** -0.5
    pool_w = jax.random.normal(ks[4], (DEPTH, POOL_GROUPS, POOL_GROUP_DIM, POOL_GROUP_DIM), f32) * POOL_GROUP_DIM ** -0.5
    pool_scale = 1.0 + 0.02 * jax.random.normal(ks[5], (DEPTH, POOL_WIDTH), f32)
    conv_w = jax.random.normal(ks[6], (DEPTH, CONV_WIDTH, LRU_WIDTH), f32) * CONV_WIDTH ** -0.5
    conv_b = 0.01 * jax.random.normal(ks[7], (DEPTH, LRU_WIDTH), f32)
    gate_a_w = jax.random.normal(ks[8], (DEPTH, LRU_HEADS, LRU_HEAD_DIM, LRU_HEAD_DIM), f32) * LRU_HEAD_DIM ** -0.5
    gate_a_b = 0.01 * jax.random.normal(ks[9], (DEPTH, LRU_HEADS, LRU_HEAD_DIM), f32)
    gate_x_w = jax.random.normal(ks[10], (DEPTH, LRU_HEADS, LRU_HEAD_DIM, LRU_HEAD_DIM), f32) * LRU_HEAD_DIM ** -0.5
    gate_x_b = 0.01 * jax.random.normal(ks[11], (DEPTH, LRU_HEADS, LRU_HEAD_DIM), f32)
    u = jax.random.uniform(ks[12], (DEPTH, LRU_WIDTH), f32, minval=0.9, maxval=0.999)
    s = u ** (1.0 / LRU_C)
    lru_lambda = jnp.log(s) - jnp.log1p(-s)
    w_out = jax.random.normal(ks[13], (DEPTH, D_MODEL, D_MODEL), f32) * D_MODEL ** -0.5
    norm2_g = 1.0 + 0.02 * jax.random.normal(ks[14], (DEPTH, D_MODEL), f32)
    mlp_w1 = jax.random.normal(ks[15], (DEPTH, D_MODEL, D_FF_2), f32) * D_MODEL ** -0.5
    mlp_w2 = jax.random.normal(ks[16], (DEPTH, D_FF_2, D_MODEL), f32) * D_FF_2 ** -0.5
    final_g = 1.0 + 0.02 * jax.random.normal(ks[17], (D_MODEL,), f32)
    return {"x": x, "meta_tokens": meta_tokens, "norm1_g": norm1_g, "w_in": w_in,
            "pool_w": pool_w, "pool_scale": pool_scale, "conv_w": conv_w, "conv_b": conv_b,
            "gate_a_w": gate_a_w, "gate_a_b": gate_a_b, "gate_x_w": gate_x_w, "gate_x_b": gate_x_b,
            "lru_lambda": lru_lambda, "w_out": w_out, "norm2_g": norm2_g,
            "mlp_w1": mlp_w1, "mlp_w2": mlp_w2, "final_g": final_g}

def second_block(x, meta_tokens, norm1_g, w_in, pool_w, pool_scale, conv_w, conv_b,
              gate_a_w, gate_a_b, gate_x_w, gate_x_b, lru_lambda, w_out, norm2_g,
              mlp_w1, mlp_w2, final_g):
    B = x.shape[0]
    meta = jnp.broadcast_to(meta_tokens[None].astype(x.dtype), (B, N_META, x.shape[-1]))
    h = jnp.concatenate([meta, x], axis=1)
    for l in range(DEPTH):
        u = rmsnorm_2(h, norm1_g[l])
        proj = u @ w_in[l]
        v_pool, v_lru, v_gelu, g_pool, g_lru = jnp.split(proj, IN_SPLITS, axis=-1)
        pool_out = pool_mixer(v_pool, pool_w[l], pool_scale[l])
        xc = causal_depthwise_conv(v_lru, conv_w[l], conv_b[l])
        lru_out = rg_lru(xc, gate_a_w[l], gate_a_b[l], gate_x_w[l], gate_x_b[l],
                         lru_lambda[l]) * jax.nn.gelu(v_gelu)
        merged = jax.nn.sigmoid(g_pool) * pool_out + jax.nn.sigmoid(g_lru) * lru_out
        h = h + merged @ w_out[l]
        u2 = rmsnorm_2(h, norm2_g[l])
        h = h + jnp.square(jax.nn.relu(u2 @ mlp_w1[l])) @ mlp_w2[l]
    out = rmsnorm_2(h, final_g)
    return out[:, N_META:]


def setup_inputs(seed=0):
    out = dict(first_inputs(seed))
    for name, value in second_inputs(seed + 1).items():
        if name != "x":
            out[name + "_2"] = value
    return out


def reference(
    x, norm_mix_g, w_in, b_in, mlstm_head_g, w_branch_m, conv_w, w_branch_c, w_out, norm_ffn_g,
    w_up, ffn_conv_w, ffn_conv_b, w_down, norm_out_g, meta_tokens_2, norm1_g_2, w_in_2,
    pool_w_2, pool_scale_2, conv_w_2, conv_b_2, gate_a_w_2, gate_a_b_2, gate_x_w_2, gate_x_b_2,
    lru_lambda_2, w_out_2, norm2_g_2, mlp_w1_2, mlp_w2_2, final_g_2,
):
    x = first_block(
        x, norm_mix_g, w_in, b_in, mlstm_head_g, w_branch_m, conv_w, w_branch_c, w_out,
        norm_ffn_g, w_up, ffn_conv_w, ffn_conv_b, w_down, norm_out_g,
    )
    return second_block(
        x, meta_tokens_2, norm1_g_2, w_in_2, pool_w_2, pool_scale_2, conv_w_2, conv_b_2,
        gate_a_w_2, gate_a_b_2, gate_x_w_2, gate_x_b_2, lru_lambda_2, w_out_2, norm2_g_2,
        mlp_w1_2, mlp_w2_2, final_g_2,
    )


_drawn_inputs = setup_inputs


def setup_inputs(seed=0):
    import zlib

    import numpy as np

    out = dict(_drawn_inputs(seed))
    spreads = {}
    factors = {'mlstm_head_g': 8.0,
     'norm_ffn_g': 3.693,
     'ffn_conv_b': 3.738,
     'norm1_g_2': 5.058,
     'pool_scale_2': 18.8,
     'conv_b_2': 12.913,
     'gate_a_b_2': 200.0,
     'gate_x_b_2': 200.0,
     'norm2_g_2': 14.487,
     'final_g_2': 22.031}
    for name, (base, spread) in spreads.items():
        noise = np.random.default_rng([zlib.crc32(name.encode()), seed]).standard_normal(out[name].shape)
        drawn = base * np.exp(spread * noise) if base else spread * noise
        out[name] = __import__('jax').numpy.asarray(drawn.astype(out[name].dtype))
    for name, factor in factors.items():
        out[name] = (out[name] * factor).astype(out[name].dtype)
    return out
```

```python
import concourse.bass as bass
from concourse import mybir
from contextlib import ExitStack

F32 = mybir.dt.float32
F32R = mybir.dt.float32r
ALU = mybir.AluOpType
ACT = mybir.ActivationFunctionType
AX = mybir.AxisListType
ds = bass.ds

P = 128
D = 2048
T = 256
NT = D // P
META = 16
TM = META + T
GW = 4
CK = 4
NC = GW * P
HALF = CK // 2 * NC
RAW = 4
SLOTS = 4
AHEAD = 3
HEADS, DQK, DV = 4, 128, 256
GATE_COL = 3072
FF_TILES = 43
FF2_TILES = 64
LRU_TILES = NT
EPS = 1e-6
NEG = -1e30


class Phase:

    def __init__(self, name, groups, chunks, unroll=False):
        self.name, self.groups, self.chunks, self.unroll = name, groups, chunks, unroll
        self.bodies = groups // 2


def plan():
    names = [
        ("qkvo", 6, 4), ("conv_in", 6, 4), ("mix_gate", 8, 4),
        ("branch_m", 4, 2), ("branch_c", 4, 2), ("out1", 4, 4),
        ("up_0", 8, 4), ("down_0", 4, 4), ("up_1", 8, 4), ("down_1", 4, 4),
        ("up_2", 4, 4), ("up_3", 2, 4), ("down_2", 4, 3),
        ("lru_in", 4, 4), ("pool_in", 4, 4), ("lru_gates", 8, 0.5), ("gelu", 4, 4),
        ("pool_mix", 4, 1), ("pool_gate", 4, 4), ("lru_gate", 4, 4), ("out2", 4, 4),
    ]
    for q in range(4):
        names += [(f"mlp1_{q}", 4, 4), (f"mlp2_{q}", 4, 4)]
    unrolled = ("down_2", "pool_mix", "lru_gates", "pool_in", "up_3")
    phases, g, c = {}, 0, 0
    for name, groups, chunks in names:
        ph = Phase(name, groups, chunks, name in unrolled)
        ph.g0, ph.c0 = g, c
        g += groups
        c += int(groups * chunks)
        assert g % 2 == 0 and c % RAW == 0
        phases[name] = ph
    return phases, g, c


STAGES = [
    [("norm_mix_g", 16), ("b_in_a", 24), ("b_in_b", 56), ("mlstm_head_g", 8), ("norm_ffn_g", 16)],
    [("ffn_conv_b", 86), ("conv_w", 24), ("norm_out_g", 16)],
    [("ffn_w0", 86), ("norm1_g_2", 16), ("pool_scale_2", 16)],
    [("ffn_w1", 86), ("conv_b_2", 16), ("norm2_g_2", 16)],
    [("ffn_w2", 86), ("lru_lambda_2", 16), ("final_g_2", 16)],
    [("conv_w_2", 64), ("gate_a_b_2", 16), ("gate_x_b_2", 16)],
]
COLUMN = {}
for _s, _rows in enumerate(STAGES):
    _at = 0
    for _name, _n in _rows:
        COLUMN[_name] = (_s * P + _at, _n)
        _at += _n


def build(nc, a, out):
    PH, GROUPS, CHUNKS = plan()
    ctx = ExitStack()
    with ctx:
        def sb(name, shape, dt=F32, stack=ctx):
            return stack.enter_context(nc.sbuf_tensor(name, shape, dt))

        sems = {}

        def sem(name):
            if name not in sems:
                sems[name] = ctx.enter_context(nc.semaphore(name))
            return sems[name]

        raw = sb("raw", [P, RAW, CK * NC])
        whi = sb("whi", [P, SLOTS, HALF], F32R)
        wlo = sb("wlo", [P, SLOTS, HALF], F32R)
        h = sb("h", [P, NT, T])
        hn = sb("hn", [P, NT, META + 2 * T], F32R)
        act = sb("act", [P, NT, 2 * T], F32R)
        meta_lo = sb("meta_lo", [P, NT, META], F32R)
        lowc = sb("lowc", [P, GW, T])
        cols = sb("cols", [P, len(STAGES) * P])
        ident = sb("ident", [P, P])
        ones = sb("ones", [P, T])
        eps = sb("eps", [P, 1])
        rstd = sb("rstd", [P, T])
        sp8 = sb("sp8", [P, NT])
        work = sb("work", [P, 8752])
        with ExitStack() as early:
            lo2 = sb("lo2", [P, NT, TM], F32R, early)
        misc = sb("misc", [P, NT * TM])

        psum = ctx.enter_context(nc.psum_tensor("psum", [P, 8, 512], F32))

        def view(t, at, *shape):
            n = 1
            for s in shape:
                n *= s
            v = t[:, at:at + n]
            if len(shape) == 2:
                v = v.rearrange("p (a b) -> p a b", b=shape[1])
            return v

        def col(name, i=0):
            return cols[:, COLUMN[name][0] + i:COLUMN[name][0] + i + 1]

        def dcol(name, i):
            return cols[:, ds(COLUMN[name][0] + i, 1)]

        ysum = view(work, 4112, GW, T)
        normed = [view(work, 5136, GW, T), view(work, 6160, GW, T)]
        squares = normed[1]
        part = view(work, 7184, 4, T)
        my = view(misc, 0, GW, T)
        ms = view(misc, 1024, GW, T)
        mt = view(misc, 2048, GW, T)
        x_nat = view(work, 0, 2, D)
        meta_nat = misc[0:META, 0:D]
        meta_sq = misc[0:META, D:2 * D]
        meta_ss = misc[0:META, 2 * D:2 * D + 2]
        stage = view(work, 4112, len(STAGES), P)
        wif = view(work, 8208, NT, 8)
        qkvo = view(work, 0, 24, T)
        v_tok = view(work, 6144, 2, HEADS * DV)
        conv_in = view(work, 0, 24, T)
        conv_pad = view(work, 6144, 8, T + 2)
        mix_gate = view(work, 0, 32, T)
        up_pad = [view(work, 0, GW, T + 2), view(work, 1032, GW, T + 2)]
        up_conv = [view(work, 2064, GW, T), view(work, 3088, GW, T)]
        lru_pad = view(work, 0, NT, TM + 3)
        pool_v = view(work, 0, NT, TM)
        xc = view(work, 4400, NT, TM)
        out_nat = view(work, 0, 2, D)
        act_flat = act[:, :, :].rearrange("p a b -> p (a b)")
        xc_parts = [view(act_flat, j * GW * 2 * TM, GW, 2 * TM) for j in range(2)]
        row_a, row_b, row_c, row_guard = [lowc[0:HEADS, j, :] for j in range(4)]
        logits = misc[0:2 * HEADS, 4096:4352]
        decay = view(misc, 0, HEADS, T + P)
        scores = view(misc, 1536, HEADS, T + P)
        num_sq = [view(misc, 3072 + 512 * j, 2, T) for j in range(2)]
        factor = view(misc, 0, HEADS, T)
        ccol = sb("ccol", [P, 2, HEADS])
        gate_b = sb("gate_b", [2 * HEADS, 1])
        z_q, i_q, a_q, w_q = [view(misc, j * GW * TM, GW, TM) for j in range(4)]
        lam = [sb(f"lam_{j}", [P, NT]) for j in range(4)]

        mask = work[:, 8336:8336 + T]
        onecol = sb("onecol", [P, HEADS, HEADS])

        chunk_loaded = [sem(f"chunk_loaded_{r}") for r in range(RAW)]
        hi_ready, lo_ready, half_used = sem("hi_ready"), sem("lo_ready"), sem("half_used")
        low_copied, psum_freed = sem("low_copied"), sem("psum_freed")
        STARTS_AT_ONE = ("h_added", "mixed_m", "merged", "lru_out", "ff_split", "mlp_split")
        C_GATES = PH["lru_gates"].c0

        NO_LOW = ("lru_in", "pool_in", "lru_gates")
        n = 0
        for ph in PH.values():
            ph.lc0 = n
            if ph.name not in NO_LOW:
                n += ph.groups

        def loaded_value(c4, gates):
            return 16 * (c4 + 1) + (16 if gates else 0)

        def by_tiles(w):
            return w.rearrange("(k p) n -> p k n", p=P)

        W_in, W_in2 = by_tiles(a["w_in"]), by_tiles(a["w_in_2"][0])
        W_bm, W_bc = by_tiles(a["w_branch_m"]), by_tiles(a["w_branch_c"])
        W_o, W_o2 = by_tiles(a["w_out"]), by_tiles(a["w_out_2"][0])
        W_up, W_down = by_tiles(a["w_up"]), by_tiles(a["w_down"])
        W_m1, W_m2 = by_tiles(a["mlp_w1_2"][0]), by_tiles(a["mlp_w2_2"][0])
        W_pool = [by_tiles(a["pool_w_2"][0, g]) for g in range(4)]
        W_ga = a["gate_a_w_2"][0].rearrange("h (k p) n -> p (h k) n", p=P)
        W_gx = a["gate_x_w_2"][0].rearrange("h (k p) n -> p (h k) n", p=P)

        SOURCE = {
            "qkvo": (W_in, 0, 0), "conv_in": (W_in, 0, 3080), "mix_gate": (W_in, 0, 6152),
            "branch_m": (W_bm, 0, 0), "branch_c": (W_bc, 0, 0), "out1": (W_o, 0, 0),
            "down_0": (W_down, 0, 0), "down_1": (W_down, 16, 0), "down_2": (W_down, 32, 0),
            "lru_in": (W_in2, 0, D), "pool_in": (W_in2, 0, 0), "gelu": (W_in2, 0, 2 * D),
            "pool_gate": (W_in2, 0, 3 * D), "lru_gate": (W_in2, 0, 4 * D), "out2": (W_o2, 0, 0),
        }
        for q in range(4):
            SOURCE[f"mlp1_{q}"] = (W_m1, 0, q * D)
            SOURCE[f"mlp2_{q}"] = (W_m2, q * NT, 0)
        UP_FIRST = {"up_0": 0, "up_1": 16, "up_2": 32, "up_3": 40}

        block = ctx.enter_context(nc.Block())

        def HB(ph):
            return int(4 * ph.chunks)

        def chunk_value(ph, i, loc):
            if isinstance(i, int):
                half = 2 * ph.c0 + HB(ph) * i + loc
                return 16 * (half // 2 // RAW + 1) + (16 if half // 2 >= C_GATES else 0)
            first = ph.c0 // RAW + (HB(ph) // 2 // RAW) * i
            return 16 * (first + loc // 2 // RAW + 1) + (16 if ph.c0 >= C_GATES else 0)

        def last_of_all(ph, i, loc):
            return 2 * ph.c0 + HB(ph) * i + loc >= 2 * CHUNKS

        final_phase = PH["mlp2_3"]

        def half_number(ph, i, loc):
            return 2 * ph.c0 + HB(ph) * i + loc if isinstance(i, int) else loc

        def loop(eng, ph, body):
            if ph.unroll or ph is final_phase:
                for i in range(ph.bodies):
                    body(i)
            else:
                with eng.Fori(0, ph.bodies) as i:
                    body(i)

        STAGE_DMAS = sum(len(r) for r in STAGES)

        @block.sync
        def _(sp):
            sp.dma_start(x_nat, a["x"][0].rearrange("(t p) n -> p t n", p=P)).then_inc(sem("x_loaded"), 16)

            def load(c, c_slot, dst_cols, src):
                if not (isinstance(c, int) and c < RAW):
                    sp.wait_ge(lo_ready, 2 * c - 2 * RAW + 2)
                kt, n = src.shape[1], src.shape[2]
                dst = raw[:, c_slot % RAW, :].rearrange("p (k n) -> p k n", n=dst_cols)[:, 0:kt, 0:n]
                sp.dma_start(dst, src).then_inc(chunk_loaded[c_slot % RAW], 16)

            def load_group(ph, body, i, s):
                nch = ph.chunks
                per_body = 2 * nch
                if ph.name.startswith("up"):
                    tiles = 3 if ph.name == "up_3" else GW
                    first = UP_FIRST[ph.name] * P + s * FF_TILES * P
                    w, k0, c_first = W_up, 0, first
                    column, n = c_first + i * NC, tiles * P
                else:
                    w, k0, c_first = SOURCE[ph.name]
                    column, n = c_first + (2 * i + s) * NC, NC
                for j in range(nch):
                    kt = min(CK, w.shape[1] - k0 - CK * j)
                    cl = s * nch + j
                    load(ph.c0 + per_body * i + cl, cl + (body * per_body if ph.unroll else 0), NC,
                         w[:, k0 + CK * j:k0 + CK * j + kt, ds(column, n)])

            for ph in PH.values():
                if ph.name == "lru_gates":
                    for q in range(4):
                        sp.wait_ge(lo_ready, 2 * (ph.c0 + q) - 2 * RAW + 2)
                        for s, w in enumerate((W_ga, W_gx)):
                            sp.dma_start(raw[:, q, s * HALF:(s + 1) * HALF].rearrange("p (k n) -> p k n", n=256),
                                         w[:, 4 * q:4 * q + 4, :]).then_inc(chunk_loaded[q], 16)
                elif ph.name == "pool_mix":
                    for g in range(4):
                        load(ph.c0 + g, g, NC, W_pool[g])
                elif ph.unroll or ph.name == "qkvo":
                    for i in range(ph.bodies):
                        for s in range(2):
                            load_group(ph, i, i, s)
                else:
                    with sp.Fori(0, ph.bodies) as i:
                        for s in range(2):
                            load_group(ph, 0, i, s)

            for t in range(2):
                sp.wait_ge(sem("out_copied"), 4 * t + 4)
                sp.dma_start(out[0, t * P:(t + 1) * P, :], out_nat[:, t, :]).then_inc(sem("out_stored"), 16)
            sp.wait_ge(sem("out_stored"), 32)

        @block.gpsimd
        def _(pool):
            pool.memset(ident[:, :], 0.0).then_inc(sem("const_cleared"), 1)
            pool.memset(mask, 0.0).then_inc(sem("const_cleared"), 1)
            pool.memset(onecol[:, :, :], 0.0).then_inc(sem("const_cleared"), 1)
            pool.memset(ones[:, :], 1.0).then_inc(sem("ones_ready"), 1)
            pool.memset(eps[:, :], EPS).then_inc(sem("ones_ready"), 1)
            pool.wait_ge(sem("const_cleared"), 3)
            pool.affine_select(out=ident[:, :], in_=ident[:, :], compare_op=ALU.not_equal, fill=1.0,
                               base=0, pattern=[[-1, P]], channel_multiplier=1).then_inc(sem("consts_ready"), 1)
            pool.affine_select(out=mask, in_=mask, compare_op=ALU.is_ge, fill=NEG,
                               base=0, pattern=[[1, T]], channel_multiplier=-1).then_inc(sem("consts_ready"), 1)
            pool.affine_select(out=onecol[:, :, :], in_=onecol[:, :, :], compare_op=ALU.not_equal, fill=1.0,
                               base=0, pattern=[[1, HEADS], [-1, HEADS]], channel_multiplier=0).then_inc(sem("consts_ready"), 1)

        @block.tensor
        def _(pe):
            mm = nc.tensor.matmul
            pe.sem_inc(half_used, 1)

            def spread_row(hd):
                return ident[0:HEADS, hd:hd + 1].to_broadcast([HEADS, P])

            pe.wait_ge(sem("consts_ready"), 3)
            pe.wait_ge(sem("stage_loaded"), STAGE_DMAS * 16)
            for s, rows in enumerate(STAGES):
                nr = sum(n for _, n in rows)
                last = nc.tensor.transpose(psum[:, 4 + s // 4, (s % 4) * P:(s % 4) * P + nr],
                                           stage[0:nr, s, :], ident[0:nr, 0:nr])
            last.then_inc(sem("cols_turned"), 1)
            pe.wait_ge(sem("x_loaded"), 16)
            for b in range(8):
                if b in (4, 5):
                    pe.wait_ge(sem("cols_copied"), b - 3)
                for f in range(2):
                    for t in range(2):
                        last = nc.tensor.transpose(psum[:, b, f * T + t * P:f * T + (t + 1) * P],
                                                   x_nat[:, t, (2 * b + f) * P:(2 * b + f + 1) * P], ident[:, :])
                last.then_inc(sem("x_turned"), 1)
            pe.wait_ge(sem("meta_normed"), 1)
            pe.wait_ge(sem("x_copied"), 8)
            for f in range(NT):
                last = nc.tensor.transpose(psum[:, 6, f * META:(f + 1) * META],
                                           meta_nat[:, f * P:(f + 1) * P], ident[0:META, 0:META])
            last.then_inc(sem("meta_turned"), 1)

            def norm_total(n):
                pe.wait_ge(sem("squares_summed"), 4 * n + 4)
                for q in range(4):
                    last = mm(psum[:, 0, 0:T], ones[:, 0:P], part[:, q, :], start=(q == 0), stop=(q == 3))
                last.then_inc(sem("norm_total"), 1)

            def group(ph, i, s, body, rhs, kts, tiles=GW, waits=()):
                g = ph.g0 + 2 * i + s
                pe.wait_ge(psum_freed, g + 1)
                nh = int(2 * ph.chunks)
                for k in range(nh):
                    if k % 2 == 0 and k // 2 < len(waits):
                        pe.wait_ge(*waits[k // 2])
                    hl = s * nh + k + (body * 2 * nh)
                    pe.wait_ge(lo_ready, 2 * ph.c0 + (2 * nh) * i + s * nh + k + 1)
                    hi = whi[:, hl % SLOTS, :].rearrange("p (k n) -> p k n", n=NC)
                    lo = wlo[:, hl % SLOTS, :].rearrange("p (k n) -> p k n", n=NC)
                    for kk in range(2):
                        kt = 2 * k + kk
                        if kt >= kts:
                            continue
                        both = rhs(kt)
                        first, end = kt == 0, kt == kts - 1
                        for m in range(tiles):
                            o = psum[:, 4 * s + m, :]
                            wide = lambda: mm(o, hi[:, kk, m * P:(m + 1) * P], both, start=first, stop=end)
                            narrow = lambda: mm(o[:, 0:T], lo[:, kk, m * P:(m + 1) * P], both[:, 0:T],
                                                start=False, stop=False)
                            if first:
                                wide()
                                last = narrow()
                            else:
                                narrow()
                                last = wide()
                    last.then_inc(half_used, 1)

            def group_wide(ph, i, s, body):
                g = ph.g0 + 2 * i + s
                pe.wait_ge(psum_freed, g + 1)
                nh = int(2 * ph.chunks)
                for k in range(nh):
                    hl = s * nh + k + (body * 2 * nh)
                    pe.wait_ge(lo_ready, 2 * ph.c0 + (2 * nh) * i + s * nh + k + 1)
                    hi = whi[:, hl % SLOTS, :].rearrange("p (k n) -> p k n", n=NC)
                    lo = wlo[:, hl % SLOTS, :].rearrange("p (k n) -> p k n", n=NC)
                    for kk in range(2):
                        kt = 2 * k + kk
                        for m in range(GW):
                            o = psum[:, 4 * s + m, 0:TM]
                            w = slice(m * P, (m + 1) * P)
                            mm(o, hi[:, kk, w], hn[:, kt, 0:TM], start=(kt == 0), stop=False)
                            mm(o, hi[:, kk, w], lo2[:, kt, :], start=False, stop=False)
                            last = mm(o, lo[:, kk, w], hn[:, kt, 0:TM], start=False, stop=(kt == NT - 1))
                    last.then_inc(half_used, 1)

            def run(name, rhs, kts=NT, tiles=(GW, GW), waits=()):
                ph = PH[name]
                if ph.unroll:
                    for i in range(ph.bodies):
                        for s in range(2):
                            group(ph, i, s, i, rhs, kts, tiles[s], waits)
                else:
                    with pe.Fori(0, ph.bodies) as i:
                        for s in range(2):
                            group(ph, i, s, 0, rhs, kts, tiles[s], waits)

            def from_hn(kt):
                return hn[:, kt, META:META + 2 * T]

            def norm_waits(n):
                return [(sem("norm_split"), 4 * n + q + 1) for q in range(4)]

            norm_total(0)
            pe.wait_ge(sem("gates_loaded"), 16)
            for q in range(4):
                pe.wait_ge(sem("norm_made"), q + 1)
                for k in range(4):
                    kt = 4 * q + k
                    last = mm(psum[0:8, 7, 0:T], wif[:, kt, :], normed[q % 2][:, k, :], start=(kt == 0), stop=(kt == NT - 1))
                last.then_inc(sem("if_used"), 1)
            run("qkvo", from_hn, waits=norm_waits(0))

            pe.wait_ge(psum_freed, PH["conv_in"].g0 + 2)
            mm(psum[0:HEADS, 4, 0:T], ident[0:8, HEADS:8], logits, start=True, stop=True)\
                .then_inc(sem("f_moved"), 1)
            for t in range(2):
                for j in range(2):
                    for f in range(4):
                        last = nc.tensor.transpose(psum[:, 2 * t + j, f * P:(f + 1) * P],
                                                   qkvo[:, 8 + 4 * j + f, t * P:(t + 1) * P], ident[:, :])
                    last.then_inc(sem("v_turned"), 1)
            pe.wait_ge(sem("m_ready"), 1)
            for t in range(2):
                last = nc.tensor.transpose(psum[:, 6, t * HEADS:(t + 1) * HEADS],
                                           row_c[:, t * P:(t + 1) * P], ident[0:HEADS, 0:HEADS])
            last.then_inc(sem("c_turned"), 1)
            for hd in range(HEADS):
                last = mm(psum[:, 4 + hd // 2, hd % 2 * T:(hd % 2 + 1) * T], spread_row(hd), row_b,
                          start=True, stop=True)
            last.then_inc(sem("m_spread"), 1)

            def score(hd):
                if hd == 0:
                    pe.wait_ge(sem("z_made"), 1)
                if hd >= 2:
                    pe.wait_ge(sem("st_made"), hd - 1)
                o = psum[:, 6 + hd % 2, :]
                mm(o[:, 0:T], qkvo[:, 4 + hd, 0:P], qkvo[:, hd, :], start=True, stop=True)
                mm(o[:, T:T + P], qkvo[:, 4 + hd, P:T], qkvo[:, hd, P:T], start=True, stop=True)\
                    .then_inc(sem("scores_made"), 1)

            def squares_of(hd):
                pe.wait_ge(sem("num_squared"), hd + 1)
                for v in range(2):
                    last = mm(psum[0:HEADS, 5, 0:T], onecol[:, hd, :], num_sq[hd % 2][:, v, :],
                              start=(hd == 0 and v == 0), stop=(hd == HEADS - 1 and v == 1))
                last.then_inc(sem("squares_used"), 1)

            score(0)
            score(1)
            pe.wait_ge(sem("v_copied"), 4)
            for hd in range(HEADS):
                pe.wait_ge(sem("st_made"), hd + 1)
                for v in range(2):
                    o = psum[:, hd, v * T:(v + 1) * T]
                    c = slice(hd * DV + v * P, hd * DV + (v + 1) * P)
                    mm(o, v_tok[:, 0, c], scores[:, hd, 0:T], start=True, stop=False)
                    last = mm(o[:, P:T], v_tok[:, 1, c], scores[:, hd, T:T + P], start=False, stop=True)
                last.then_inc(sem("num_made"), 1)
                mm(psum[0:HEADS, 4, 0:T], onecol[:, hd, :], scores[:, hd, 0:T], start=(hd == 0), stop=False)
                mm(psum[0:HEADS, 4, P:T], onecol[:, hd, :], scores[:, hd, T:T + P], start=False,
                   stop=(hd == HEADS - 1)).then_inc(sem("den_made"), 1)
                if hd + 2 < HEADS:
                    score(hd + 2)
                if hd >= 1:
                    squares_of(hd - 1)
            squares_of(HEADS - 1)
            pe.wait_ge(sem("factor_made"), 1)
            for hd in range(HEADS):
                last = mm(psum[:, 6 + hd // 2, hd % 2 * T:(hd % 2 + 1) * T], spread_row(hd), row_a,
                          start=True, stop=True)
            last.then_inc(sem("factor_spread"), 1)
            pe.wait_ge(sem("hm_scaled"), 8)

            run("conv_in", from_hn)
            run("mix_gate", from_hn)
            run("branch_m", lambda kt: act[:, kt, :], kts=8, waits=[(sem("hm_split"), 1), (sem("hm_split"), 2)])
            run("branch_c", lambda kt: act[:, 8 + kt, :], kts=8, waits=[(sem("conv_split"), 1), (sem("conv_split"), 2)])
            run("out1", from_hn, waits=[(sem("merged_split"), q + 1) for q in range(4)])
            norm_total(1)
            from_act = lambda kt: act[:, kt, :]
            run("up_0", from_hn, waits=norm_waits(1))
            run("down_0", from_act, waits=[(sem("ff_split"), 1 + q + 1) for q in range(4)])
            run("up_1", from_hn)
            run("down_1", from_act, waits=[(sem("ff_split"), 1 + q + 5) for q in range(4)])
            run("up_2", from_hn)
            run("up_3", from_hn, tiles=(3, 3))
            run("down_2", from_act, kts=11, waits=[(sem("ff_split"), 1 + q + 9) for q in range(3)])
            norm_total(2)
            norm_total(3)

            for q in range(4):
                pe.wait_ge(sem("norm_split"), 4 * 2 + q + 1)
            pe.wait_ge(sem("lo2_made"), 5)
            for name in ("lru_in", "pool_in"):
                ph = PH[name]
                if ph.unroll:
                    for i in range(ph.bodies):
                        for s in range(2):
                            group_wide(ph, i, s, i)
                else:
                    with pe.Fori(0, ph.bodies) as i:
                        for s in range(2):
                            group_wide(ph, i, s, 0)
            ph = PH["lru_gates"]
            for q in range(4):
                pe.wait_ge(sem("xc_split"), q + 1)
                xq = xc_parts[q % 2]
                for s in range(2):
                    g = ph.g0 + 2 * q + s
                    pe.wait_ge(psum_freed, g + 1)
                    H = 2 * ph.c0 + 2 * q + s
                    pe.wait_ge(lo_ready, H + 1)
                    hi = whi[:, H % SLOTS, :].rearrange("p (h k n) -> p h k n", h=2, k=2)
                    lo = wlo[:, H % SLOTS, :].rearrange("p (h k n) -> p h k n", h=2, k=2)
                    for m in range(GW):
                        o = psum[:, 4 * s + m, 0:TM]
                        w = slice(m % 2 * P, (m % 2 + 1) * P)
                        for k in range(2):
                            kt = 2 * (m // 2) + k
                            mm(o, hi[:, m // 2, k, w], xq[:, kt, 0:TM], start=(k == 0), stop=False)
                            mm(o, hi[:, m // 2, k, w], xq[:, kt, TM:2 * TM], start=False, stop=False)
                            last = mm(o, lo[:, m // 2, k, w], xq[:, kt, 0:TM], start=False, stop=(k == 1))
                    last.then_inc(half_used, 1)
            run("gelu", from_hn)
            ph = PH["pool_mix"]
            for i in range(2):
                for s in range(2):
                    g4 = 2 * i + s
                    group(ph, i, s, i, lambda kt: act[:, 4 * g4 + kt, :], 4, waits=[(sem("pool_split"), g4 + 1)])
            run("pool_gate", from_hn)
            run("lru_gate", from_hn)
            run("out2", from_act, waits=[(sem("merged2_split"), q + 1) for q in range(4)])
            norm_total(4)
            for q in range(4):
                run(f"mlp1_{q}", from_hn, waits=norm_waits(3) if q == 0 else ())
                run(f"mlp2_{q}", from_act, waits=[(sem("mlp_split"), 1 + 4 * q + j + 1) for j in range(4)])
            norm_total(5)
            for t in range(2):
                for q in range(4):
                    pe.wait_ge(sem("final_made"), q + 1)
                    for f in range(4):
                        last = nc.tensor.transpose(psum[:, 4 * t + q, f * P:(f + 1) * P],
                                                   h[:, 4 * q + f, t * P:(t + 1) * P], ident[:, :])
                    last.then_inc(sem("out_turned"), 1)

        @block.scalar
        def _(ac):
            A = nc.scalar.activation

            def rows(src, r):
                return src.rearrange("(r p) -> r p", p=P)[0:r, :]

            source = {
                "norm_mix_g": a["norm_mix_g"], "b_in_a": a["b_in"][0:GATE_COL], "b_in_b": a["b_in"][GATE_COL + 8:],
                "mlstm_head_g": a["mlstm_head_g"], "norm_ffn_g": a["norm_ffn_g"], "ffn_conv_b": a["ffn_conv_b"],
                "norm_out_g": a["norm_out_g"], "ffn_w0": a["ffn_conv_w"][0], "ffn_w1": a["ffn_conv_w"][1],
                "ffn_w2": a["ffn_conv_w"][2], "norm1_g_2": a["norm1_g_2"][0], "pool_scale_2": a["pool_scale_2"][0],
                "conv_b_2": a["conv_b_2"][0], "norm2_g_2": a["norm2_g_2"][0], "lru_lambda_2": a["lru_lambda_2"][0],
                "final_g_2": a["final_g_2"],
                "conv_w": a["conv_w"].rearrange("k (r p) -> (k r) p", p=P),
                "conv_w_2": a["conv_w_2"][0].rearrange("k (r p) -> (k r) p", p=P),
                "gate_a_b_2": a["gate_a_b_2"][0].rearrange("h (r p) -> (h r) p", p=P),
                "gate_x_b_2": a["gate_x_b_2"][0].rearrange("h (r p) -> (h r) p", p=P),
            }
            ac.dma_start(meta_nat, a["meta_tokens_2"]).then_inc(sem("meta_loaded"), 16)
            for s, rws in enumerate(STAGES):
                at = 0
                for name, n in rws:
                    src = source[name]
                    if len(src.shape) == 1:
                        src = rows(src, n)
                    ac.dma_start(stage[at:at + n, s, :], src).then_inc(sem("stage_loaded"), 16)
                    at += n
            ac.dma_start(wif, by_tiles(a["w_in"])[:, :, GATE_COL:GATE_COL + 8]).then_inc(sem("gates_loaded"), 16)
            ac.dma_start(gate_b[:, :], a["b_in"][GATE_COL:GATE_COL + 8].rearrange("(r o) -> r o", o=1))\
                .then_inc(sem("gate_b_loaded"), 16)

            def split(ph, i, loc):
                hc = 2 * ph.c0 + HB(ph) * i + loc
                n = half_number(ph, i, loc)
                ac.wait_ge(chunk_loaded[n // 2 % RAW], chunk_value(ph, i, loc))
                if not (isinstance(hc, int) and hc < SLOTS):
                    ac.wait_ge(half_used, 1 + hc - SLOTS + 1)
                A(whi[:, n % SLOTS, :], raw[:, n // 2 % RAW, n % 2 * HALF:(n % 2 + 1) * HALF], ACT.Copy)\
                    .then_inc(hi_ready, 1)

            def splits(ph, i, s):
                n = HB(ph) // 2
                for k in range(n):
                    loc = AHEAD + s * n + k
                    if not isinstance(i, int) or not last_of_all(ph, i, loc):
                        split(ph, i, loc)

            def low(ph, i, s, bias=None, tiles=GW):
                ac.wait_ge(half_used, 1 + HB(ph) * i + 2 * ph.c0 + (s + 1) * (HB(ph) // 2))
                ac.wait_ge(psum_freed, ph.g0 + 2 * i + s + 2)
                if bias is None:
                    A(lowc[:, 0:tiles, :], psum[:, 4 * s:4 * s + tiles, T:2 * T], ACT.Copy).then_inc(low_copied, 1)
                else:
                    for m in range(tiles):
                        last = A(lowc[:, m, :], psum[:, 4 * s + m, T:2 * T], ACT.Identity,
                                 bias=dcol(bias[0], bias[1] + GW * (2 * i + s) + m))
                    last.then_inc(low_copied, 1)

            def run(name, bias=None, tiles=GW, after=None, wide=False):
                ph = PH[name]

                def body(i):
                    for s in range(2):
                        splits(ph, i, s)
                        if not wide:
                            low(ph, i, s, bias, tiles)
                        if after:
                            after(ph, i, s)
                loop(ac, ph, body)

            def square(n, q):
                if n or q:
                    ac.wait_ge(sem("squares_summed"), 4 * n + q)
                A(squares, h[:, 4 * q:4 * q + 4, :], ACT.Square).then_inc(sem("squared"), 1)

            def norm(n, split_at=None):
                ac.wait_ge(sem("norm_total"), n + 1)
                A(rstd[:, :], psum[:, 0, 0:T], ACT.Sqrt, bias=eps[:, 0:1], scale=1.0 / D).then_inc(sem("norm_root"), 1)
                if split_at is not None:
                    for q in range(4):
                        ac.wait_ge(sem("norm_made"), 4 * split_at + q + 1)
                        A(hn[:, 4 * q:4 * q + 4, META:META + T], normed[q % 2], ACT.Copy).then_inc(sem("norm_hi"), 1)

            ac.wait_ge(sem("meta_loaded"), 16)
            ac.wait_ge(sem("ones_ready"), 2)
            A(meta_sq, meta_nat, ACT.Square, accum_out=meta_ss[:, 0:1]).then_inc(sem("meta_squared"), 1)
            ac.wait_ge(sem("meta_squared"), 1)
            A(meta_ss[:, 1:2], meta_ss[:, 0:1], ACT.Sqrt, bias=eps[0:META, 0:1], scale=1.0 / D)\
                .then_inc(sem("meta_root"), 1)
            ac.wait_ge(sem("cols_copied"), 2)
            c0, n0 = COLUMN["lru_lambda_2"]
            A(lam[0][:, :], cols[:, c0:c0 + n0], ACT.Abs).then_inc(sem("lam_abs"), 1)
            ac.wait_ge(sem("lam_abs"), 1)
            A(lam[0][:, :], lam[0][:, :], ACT.Exp, scale=-1.0).then_inc(sem("lam_exp"), 1)
            for q in range(4):
                ac.wait_ge(sem("x_copied"), 2 * q + 2)
                square(0, q)
            for loc in range(AHEAD):
                split(PH["qkvo"], 0, loc)
            norm(0, 0)
            run("qkvo", bias=("b_in_a", 0))

            ac.wait_ge(psum_freed, PH["conv_in"].g0 + 2)
            A(qkvo[:, 16:24, :], qkvo[:, 16:24, :], ACT.Sigmoid).then_inc(sem("o_ready"), 1)
            ac.wait_ge(sem("f_copied"), 1)
            A(row_a, row_c, ACT.Abs).then_inc(sem("f_step"), 1)
            ac.wait_ge(sem("f_step"), 1)
            A(row_a, row_a, ACT.Exp, scale=-1.0).then_inc(sem("f_step"), 1)
            ac.wait_ge(sem("f_step"), 2)
            A(row_a, row_a, ACT.Ln, bias=1.0).then_inc(sem("f_step"), 1)
            ac.wait_ge(sem("guard_sum"), 1)
            A(row_guard, row_guard, ACT.Exp, scale=-1.0).then_inc(sem("guard_ready"), 1)
            ac.wait_ge(sem("z_made"), 1)
            for hd in range(HEADS):
                A(decay[:, hd, 0:T], decay[:, hd, 0:T], ACT.Exp, bias=ccol[:, 0, hd:hd + 1])
                A(decay[:, hd, T:T + P], decay[:, hd, T:T + P], ACT.Exp, bias=ccol[:, 1, hd:hd + 1])\
                    .then_inc(sem("decay_made"), 1)
            for hd in range(HEADS):
                ac.wait_ge(sem("num_made"), hd + 1)
                if hd >= 2:
                    ac.wait_ge(sem("squares_used"), hd - 1)
                A(num_sq[hd % 2], psum[:, hd, :].rearrange("p (a b) -> p a b", b=T), ACT.Square)\
                    .then_inc(sem("num_squared"), 1)
            ac.wait_ge(sem("den_made"), HEADS)
            A(row_a, psum[0:HEADS, 4, 0:T], ACT.Abs).then_inc(sem("den_abs"), 1)
            ac.wait_ge(sem("ms_made"), 1)
            A(row_b, row_b, ACT.Sqrt, bias=eps[0:HEADS, 0:1], scale=1.0 / DV).then_inc(sem("ms_root"), 1)
            ac.wait_ge(sem("factor_spread"), 1)
            A(factor, psum[:, 6:8, :].rearrange("p a (b t) -> p (a b) t", t=T), ACT.Copy).then_inc(sem("factor_copied"), 1)
            for q in range(2):
                ac.wait_ge(sem("hm_made"), q + 1)
                A(act[:, 4 * q:4 * q + 4, 0:T], qkvo[:, 4 * q:4 * q + 4, :], ACT.Copy).then_inc(sem("hm_hi"), 1)
            ac.wait_ge(sem("hm_split"), 2)

            run("conv_in", bias=("b_in_b", 0))
            for q in range(2):
                ac.wait_ge(sem("conv_prod"), q + 1)
                for m in range(GW):
                    f = 4 * q + m
                    last = A(conv_in[:, 8 + f, :], conv_pad[:, f, 2:2 + T], ACT.Copy, scale=col("conv_w", 16 + f))
                last.then_inc(sem("conv_tap"), 1)
            for q in range(2):
                ac.wait_ge(sem("conv_made"), q + 1)
                A(act[:, 8 + 4 * q:12 + 4 * q, 0:T], conv_in[:, 8 + 4 * q:12 + 4 * q, :], ACT.Copy).then_inc(sem("conv_hi"), 1)

            def mix_sigmoid(ph, i, s):
                ac.wait_ge(psum_freed, ph.g0 + 2 * i + s + 3)
                t = mix_gate[:, ds(GW * (2 * i + s), GW), :]
                A(t, t, ACT.Sigmoid).then_inc(sem("mix_gate_ready"), 1)

            run("mix_gate", bias=("b_in_b", 24), after=mix_sigmoid)
            run("branch_m")

            def merged_high(ph, i, s):
                g = 2 * i + s
                ac.wait_ge(sem("merged"), 1 + g + 1)
                A(hn[:, ds(GW * g, GW), META:META + T], mix_gate[:, ds(GW * g, GW), :], ACT.Copy)\
                    .then_inc(sem("merged_hi"), 1)

            run("branch_c", after=merged_high)

            def squares_after(base, n):
                def f(ph, i, s):
                    g = 2 * i + s
                    ac.wait_ge(sem("h_added"), 1 + base + g + 1)
                    ac.wait_ge(sem("squares_summed"), 4 * n + g)
                    A(squares, h[:, ds(GW * g, GW), :], ACT.Square).then_inc(sem("squared"), 1)
                return f

            run("out1", after=squares_after(0, 1))
            norm(1, 1)

            def up_after(first, base, tiles=GW):
                def f(ph, i, s):
                    b = base + i
                    ac.wait_ge(psum_freed, ph.g0 + 2 * i + s + 3)
                    for m in range(tiles):
                        t = s * FF_TILES + first + GW * i + m
                        last = A(up_conv[s][:, m, :], up_pad[s][:, m, 2:2 + T], ACT.Identity,
                                 bias=dcol("ffn_conv_b", t), scale=dcol("ffn_w2", t))
                    last.then_inc(sem("ff_tap"), 1)
                    if s == 0:
                        ac.wait_ge(sem("ff_conv"), 2 * b + 1)
                        A(ysum[:, 0:tiles, :], up_conv[0][:, 0:tiles, :], ACT.Sigmoid).then_inc(sem("ff_sigmoid"), 1)
                    else:
                        ac.wait_ge(sem("ff_made"), b + 1)
                        A(act[:, ds(first % 16 + GW * i, tiles), 0:T], normed[0][:, 0:tiles, :], ACT.Copy)\
                            .then_inc(sem("ff_hi"), 1)
                return f

            run("up_0", after=up_after(0, 0))
            run("down_0")
            run("up_1", after=up_after(16, 4))
            run("down_1")
            run("up_2", after=up_after(32, 8))
            run("up_3", tiles=3, after=up_after(40, 10, 3))
            run("down_2", after=squares_after(4 + 8, 2))
            norm(2)
            for q in range(4):
                ac.wait_ge(sem("block_out"), q + 1)
                square(3, q)
            norm(3, 2)

            run("lru_in", wide=True)
            for f in range(NT):
                if f == 0:
                    ac.wait_ge(psum_freed, PH["pool_in"].g0 + 2)
                A(xc[:, f, :], lru_pad[:, f, 3:3 + TM], ACT.Identity,
                  bias=col("conv_b_2", f), scale=col("conv_w_2", 3 * NT + f)).then_inc(sem("lru_tap"), 1)

            def xc_high(q):
                ac.wait_ge(sem("xc_made"), 4 * q + 4)
                if q >= 2:
                    ac.wait_ge(half_used, 1 + 2 * PH["lru_gates"].c0 + 2 * (q - 2) + 2)
                A(xc_parts[q % 2][:, :, 0:TM], xc[:, 4 * q:4 * q + 4, :], ACT.Copy).then_inc(sem("xc_hi"), 1)

            xc_high(0)
            xc_high(1)
            run("pool_in", wide=True)

            ph = PH["lru_gates"]
            for q in range(4):
                for s in range(2):
                    splits(ph, q, s)
                for s, (dst, bias) in enumerate(((z_q, "gate_a_b_2"), (i_q, "gate_x_b_2"))):
                    ac.wait_ge(half_used, 1 + 2 * ph.c0 + 2 * q + s + 1)
                    if q:
                        ac.wait_ge(sem("lru_scanned"), q)
                    for m in range(GW):
                        last = A(dst[:, m, :], psum[:, 4 * s + m, 0:TM], ACT.Sigmoid, bias=col(bias, 4 * q + m))
                    last.then_inc(sem("gate_sigmoid"), 1)
                ac.wait_ge(sem("log_a_made"), q + 1)
                A(w_q, z_q, ACT.Square).then_inc(sem("log_a_squared"), 1)
                A(a_q, z_q, ACT.Exp).then_inc(sem("a_made"), 1)
                if q + 2 < 4:
                    xc_high(q + 2)
                ac.wait_ge(sem("one_minus_a2"), q + 1)
                A(w_q, w_q, ACT.Sqrt).then_inc(sem("mult_made"), 1)
            for g in range(4):
                ac.wait_ge(sem("pool_diff"), g + 1)
                A(act[:, 4 * g:4 * g + 4, 0:T], pool_v[:, 4 * g:4 * g + 4, META:TM], ACT.Copy).then_inc(sem("pool_hi"), 1)

            def gelu(ph, i, s):
                g = 2 * i + s
                ac.wait_ge(psum_freed, ph.g0 + g + 3)
                A(ms, my, ACT.Square).then_inc(sem("gelu_square"), 1)
                ac.wait_ge(sem("gelu_inner"), 2 * g + 2)
                A(ms, ms, ACT.Sigmoid, scale=1.5957691216057308).then_inc(sem("gelu_sigmoid"), 1)

            run("gelu", after=gelu)
            run("pool_mix")

            def gate_sig(name):
                def f(ph, i, s):
                    ac.wait_ge(psum_freed, ph.g0 + 2 * i + s + 3)
                    A(ms, my, ACT.Sigmoid).then_inc(sem(name), 1)
                return f

            def lru_after(ph, i, s):
                g = 2 * i + s
                gate_sig("lru_gate_sigmoid")(ph, i, s)
                ac.wait_ge(sem("merged2"), g + 1)
                A(act[:, ds(GW * g, GW), 0:T], pool_v[:, ds(GW * g, GW), META:TM], ACT.Copy).then_inc(sem("merged2_hi"), 1)

            run("pool_gate", after=gate_sig("pool_gate_sigmoid"))
            run("lru_gate", after=lru_after)
            run("out2", after=squares_after(12 + 4, 4))
            norm(4, 3)

            def mlp_high(base):
                def f(ph, i, s):
                    g = 2 * i + s
                    ac.wait_ge(sem("mlp_made"), base + g + 1)
                    A(act[:, ds(GW * g, GW), 0:T], normed[0], ACT.Copy).then_inc(sem("mlp_hi"), 1)
                return f

            for q in range(4):
                run(f"mlp1_{q}", after=mlp_high(4 * q))
                run(f"mlp2_{q}", after=squares_after(20 + 12, 5) if q == 3 else None)
            norm(5)
            for t in range(2):
                for q in range(4):
                    ac.wait_ge(sem("out_turned"), 4 * t + q + 1)
                    A(out_nat[:, t, q * 512:(q + 1) * 512], psum[:, 4 * t + q, :], ACT.Copy).then_inc(sem("out_copied"), 1)

        @block.vector
        def _(ve):
            V = nc.vector
            for name in STARTS_AT_ONE:
                ve.sem_inc(sem(name), 1)
            chain = [0]

            def link(ins):
                chain[0] += 1
                ins.then_inc(sem("vector_chain"), 1)
                ve.wait_ge(sem("vector_chain"), chain[0])

            def split(ph, i, loc):
                n = half_number(ph, i, loc)
                ve.wait_ge(hi_ready, 2 * ph.c0 + HB(ph) * i + loc + 1)
                V.tensor_tensor(wlo[:, n % SLOTS, :], raw[:, n // 2 % RAW, n % 2 * HALF:(n % 2 + 1) * HALF],
                                whi[:, n % SLOTS, :].bitcast(F32), ALU.subtract).then_inc(lo_ready, 1)

            def splits(ph, i, s):
                n = HB(ph) // 2
                for k in range(n):
                    loc = AHEAD + s * n + k
                    if not isinstance(i, int) or not last_of_all(ph, i, loc):
                        split(ph, i, loc)

            def total(ph, i, s, dst, tiles=GW, unused=None):
                if unused is not None:
                    ve.wait_ge(*unused)
                ve.wait_ge(low_copied, ph.lc0 + 2 * i + s + 1)
                V.tensor_tensor(dst, psum[:, 4 * s:4 * s + tiles, 0:T], lowc[:, 0:tiles, :], ALU.add)\
                    .then_inc(psum_freed, 1)

            def totalled(ph, i, s):
                ve.wait_ge(psum_freed, ph.g0 + 2 * i + s + 3)

            def run(name, evac):
                ph = PH[name]

                def body(i):
                    for s in range(2):
                        splits(ph, i, s)
                        evac(ph, i, s)
                loop(ve, ph, body)

            def reduce_quarter(n, g):
                ve.wait_ge(sem("squared"), 4 * n + g + 1)
                V.tensor_reduce(part[:, ds(g, 1), :].rearrange("p o t -> p (o t)"), squares.rearrange("p k t -> p t k"),
                                AX.X, ALU.add).then_inc(sem("squares_summed"), 1)

            def low_of(dst, src, high, done):
                V.tensor_tensor(dst, src, high.bitcast(F32), ALU.subtract).then_inc(done, 1)

            H_ADDED = {1: 4, 2: 16, 4: 20, 5: 36}

            def norm(n, g_name, split_at=None, in_place=None, wide=False):
                ve.wait_ge(sem("norm_root"), n + 1)
                if n in H_ADDED:
                    ve.wait_ge(sem("h_added"), 1 + H_ADDED[n])
                if n == 0:
                    ve.sem_inc(psum_freed, 1)
                link(V.reciprocal(rstd[:, :], rstd[:, :]))
                if split_at is None:
                    for q in range(4):
                        for m in range(GW):
                            t = h[:, 4 * q + m, :]
                            last = V.scalar_tensor_tensor(t, t, col(g_name, 4 * q + m), rstd[:, :], ALU.mult, ALU.mult)
                        last.then_inc(in_place, 1)
                    return

                def make(q):
                    if q >= 2:
                        ve.wait_ge(sem("norm_split"), 4 * split_at + q - 1)
                        if n == 0:
                            ve.wait_ge(sem("if_used"), q - 1)
                    for m in range(GW):
                        last = V.scalar_tensor_tensor(normed[q % 2][:, m, :], h[:, 4 * q + m, :],
                                                      col(g_name, 4 * q + m), rstd[:, :], ALU.mult, ALU.mult)
                    last.then_inc(sem("norm_made"), 1)

                make(0)
                for q in range(4):
                    if q + 1 < 4:
                        make(q + 1)
                    ve.wait_ge(sem("norm_hi"), 4 * split_at + q + 1)
                    high = hn[:, 4 * q:4 * q + 4, META:META + T]
                    if wide:
                        low_of(lo2[:, 4 * q:4 * q + 4, META:TM], normed[q % 2], high, sem("lo2_made"))
                    low_of(hn[:, 4 * q:4 * q + 4, META + T:META + 2 * T], normed[q % 2], high, sem("norm_split"))

            ve.wait_ge(sem("cols_turned"), 1)
            for s, rws in enumerate(STAGES):
                nr = sum(n for _, n in rws)
                last = V.tensor_copy(cols[:, s * P:s * P + nr], psum[:, 4 + s // 4, (s % 4) * P:(s % 4) * P + nr])
                if s in (3, 5):
                    last.then_inc(sem("cols_copied"), 1)
            for b in range(8):
                ve.wait_ge(sem("x_turned"), b + 1)
                V.tensor_copy(h[:, 2 * b:2 * b + 2, :], psum[:, b, :].rearrange("p (f t) -> p f t", t=T))\
                    .then_inc(sem("x_copied"), 1)
            ve.wait_ge(sem("meta_root"), 1)
            link(V.reciprocal(meta_ss[:, 1:2], meta_ss[:, 1:2]))
            V.tensor_scalar(meta_nat, meta_nat, meta_ss[:, 1:2], None, ALU.mult).then_inc(sem("meta_normed"), 1)
            for q in range(4):
                ve.wait_ge(sem("squared"), q + 1)
                V.tensor_reduce(part[:, q, :], squares.rearrange("p k t -> p t k"), AX.X, ALU.add)\
                    .then_inc(sem("squares_summed"), 1)
            ve.wait_ge(sem("meta_turned"), 1)
            g1 = COLUMN["norm1_g_2"][0]
            meta_f = view(misc, 0, NT, META)
            link(V.tensor_tensor(meta_f, psum[:, 6, 0:NT * META].rearrange("p (f t) -> p f t", t=META),
                                 cols[:, g1:g1 + NT].unsqueeze(2).to_broadcast([P, NT, META]), ALU.mult))
            link(V.tensor_copy(hn[:, :, 0:META], meta_f))
            link(V.tensor_tensor(meta_lo[:, :, :], meta_f, hn[:, :, 0:META].bitcast(F32), ALU.subtract))
            ve.wait_ge(sem("lam_exp"), 1)
            e, z, zz, s_ = [t[:, :] for t in lam]
            link(V.tensor_scalar(z, e, 2.0, None, ALU.add))
            link(V.reciprocal(z, z))
            link(V.tensor_tensor(z, z, e, ALU.mult))
            link(V.tensor_tensor(zz, z, z, ALU.mult))
            link(V.tensor_scalar(s_, zz, 1.0 / 19, 1.0 / 17, ALU.mult, ALU.add))
            for k in range(7, -1, -1):
                link(V.tensor_tensor(s_, s_, zz, ALU.mult))
                link(V.tensor_scalar(s_, s_, 1.0 / (2 * k + 1), None, ALU.add))
            link(V.scalar_tensor_tensor(s_, s_, 2.0, z, ALU.mult, ALU.mult))
            c_lam = COLUMN["lru_lambda_2"][0]
            link(V.tensor_scalar(z, cols[:, c_lam:c_lam + NT], -1.0, 0.0, ALU.mult, ALU.max))
            link(V.tensor_tensor(s_, s_, z, ALU.add))
            link(V.tensor_scalar(sp8[:, :], s_, -8.0, None, ALU.mult))
            for loc in range(AHEAD):
                split(PH["qkvo"], 0, loc)
            ve.wait_ge(sem("x_copied"), 8)
            norm(0, "norm_mix_g", split_at=0)
            ve.wait_ge(sem("gate_b_loaded"), 16)
            ve.wait_ge(sem("if_used"), 4)
            V.tensor_scalar(logits, psum[0:8, 7, 0:T], gate_b[:, 0:1], None, ALU.add).then_inc(psum_freed, 1)

            run("qkvo", lambda ph, i, s: total(ph, i, s, qkvo[:, ds(GW * (2 * i + s), GW), :]))

            ve.wait_ge(sem("f_moved"), 1)
            V.tensor_copy(row_c, psum[0:HEADS, 4, 0:T]).then_inc(sem("f_copied"), 1)
            ve.wait_ge(sem("f_copied"), 1)
            link(V.tensor_scalar(row_b, row_c, 0.0, None, ALU.min))
            ve.wait_ge(sem("f_step"), 3)
            link(V.tensor_tensor(row_b, row_b, row_a, ALU.subtract))
            link(V.tensor_tensor_scan(row_a, ones[0:HEADS, 0:T], row_b, 0.0, ALU.mult, ALU.add))
            link(V.tensor_tensor(row_c, logits[0:HEADS, :], row_a, ALU.subtract))
            link(V.tensor_tensor_scan(row_b, row_c, row_c, 0.0, ALU.max, ALU.max))
            V.tensor_tensor(row_guard, row_a, row_b, ALU.add).then_inc(sem("guard_sum"), 1)
            ve.sem_inc(sem("m_ready"), 1)
            for t in range(2):
                for j in range(2):
                    ve.wait_ge(sem("v_turned"), 2 * t + j + 1)
                    V.tensor_copy(v_tok[:, t, j * 512:(j + 1) * 512], psum[:, 2 * t + j, :]).then_inc(sem("v_copied"), 1)
            ve.wait_ge(sem("c_turned"), 1)
            V.tensor_copy(ccol[:, :, :], psum[:, 6, 0:2 * HEADS].rearrange("p (a b) -> p a b", b=HEADS))
            ve.wait_ge(sem("m_spread"), 1)
            spread = psum[:, 4:6, :].rearrange("p a (b t) -> p (a b) t", t=T)
            V.scalar_tensor_tensor(decay[:, :, 0:T], spread, -1.0,
                                   mask.unsqueeze(1).to_broadcast([P, HEADS, T]), ALU.mult, ALU.add)
            V.scalar_tensor_tensor(decay[:, :, T:T + P], spread[:, :, P:T], -1.0,
                                   mask[:, 0:P].unsqueeze(1).to_broadcast([P, HEADS, P]), ALU.mult, ALU.add)\
                .then_inc(sem("z_made"), 1)
            for hd in range(HEADS):
                ve.wait_ge(sem("decay_made"), hd + 1)
                ve.wait_ge(sem("scores_made"), hd + 1)
                V.scalar_tensor_tensor(scores[:, hd, :], psum[:, 6 + hd % 2, 0:T + P], DQK ** -0.5, decay[:, hd, :],
                                       ALU.mult, ALU.mult).then_inc(sem("st_made"), 1)
            ve.wait_ge(sem("den_abs"), 1)
            ve.wait_ge(sem("guard_ready"), 1)
            link(V.tensor_tensor(row_a, row_a, row_guard, ALU.max))
            link(V.reciprocal(row_a, row_a))
            link(V.tensor_tensor(row_b, row_a, row_a, ALU.mult))
            ve.wait_ge(sem("squares_used"), HEADS)
            V.tensor_tensor(row_b, row_b, psum[0:HEADS, 5, 0:T], ALU.mult).then_inc(sem("ms_made"), 1)
            ve.wait_ge(sem("ms_root"), 1)
            link(V.reciprocal(row_b, row_b))
            V.tensor_tensor(row_a, row_a, row_b, ALU.mult).then_inc(sem("factor_made"), 1)
            ve.wait_ge(sem("factor_copied"), 1)
            ve.wait_ge(sem("o_ready"), 1)
            for f in range(8):
                V.scalar_tensor_tensor(qkvo[:, f, :], psum[:, f // 2, f % 2 * T:(f % 2 + 1) * T],
                                       col("mlstm_head_g", f), factor[:, f // 2, :], ALU.mult, ALU.mult)\
                    .then_inc(sem("hm_scaled"), 1)
            for q in range(2):
                ve.wait_ge(sem("hm_scaled"), 4 * q + 4)
                t = qkvo[:, 4 * q:4 * q + 4, :]
                V.tensor_tensor(t, t, qkvo[:, 16 + 4 * q:20 + 4 * q, :], ALU.mult).then_inc(sem("hm_made"), 1)
            for q in range(2):
                ve.wait_ge(sem("hm_hi"), q + 1)
                low_of(act[:, 4 * q:4 * q + 4, T:2 * T], qkvo[:, 4 * q:4 * q + 4, :], act[:, 4 * q:4 * q + 4, 0:T],
                       sem("hm_split"))

            ve.wait_ge(sem("hm_split"), 2)
            V.memset(conv_pad[:, :, 0:2], 0.0).then_inc(sem("conv_cleared"), 1)
            run("conv_in", lambda ph, i, s: total(ph, i, s, conv_in[:, ds(GW * (2 * i + s), GW), :]))
            totalled(PH["conv_in"], 2, 1)
            ve.wait_ge(sem("conv_cleared"), 1)
            for q in range(2):
                V.tensor_tensor(conv_pad[:, 4 * q:4 * q + 4, 2:2 + T], conv_in[:, 8 + 4 * q:12 + 4 * q, :],
                                conv_in[:, 16 + 4 * q:20 + 4 * q, :], ALU.mult).then_inc(sem("conv_prod"), 1)
            for q in range(2):
                ve.wait_ge(sem("conv_tap"), q + 1)
                for k in (1, 0):
                    for m in range(GW):
                        f = 4 * q + m
                        last = V.scalar_tensor_tensor(conv_in[:, 8 + f, :], conv_pad[:, f, k:k + T], col("conv_w", 8 * k + f),
                                                      conv_in[:, 8 + f, :], ALU.mult, ALU.add)
                    link(last)
                t = conv_in[:, 8 + 4 * q:12 + 4 * q, :]
                V.tensor_tensor(t, t, conv_in[:, 4 * q:4 * q + 4, :], ALU.mult).then_inc(sem("conv_made"), 1)
            for q in range(2):
                ve.wait_ge(sem("conv_hi"), q + 1)
                low_of(act[:, 8 + 4 * q:12 + 4 * q, T:2 * T], conv_in[:, 8 + 4 * q:12 + 4 * q, :],
                       act[:, 8 + 4 * q:12 + 4 * q, 0:T], sem("conv_split"))

            ve.wait_ge(sem("conv_split"), 2)
            run("mix_gate", lambda ph, i, s: total(ph, i, s, mix_gate[:, ds(GW * (2 * i + s), GW), :]))

            def branch_m(ph, i, s):
                g = 2 * i + s
                total(ph, i, s, my, unused=(sem("mixed_m"), 1 + g))
                totalled(ph, i, s)
                ve.wait_ge(sem("mix_gate_ready"), 8)
                t = mix_gate[:, ds(GW * g, GW), :]
                V.tensor_tensor(t, t, my, ALU.mult).then_inc(sem("mixed_m"), 1)

            run("branch_m", branch_m)

            def branch_c(ph, i, s):
                g = 2 * i + s
                ve.wait_ge(sem("mixed_m"), 1 + 4)
                total(ph, i, s, my, unused=(sem("merged"), 1 + g))
                totalled(ph, i, s)
                V.tensor_tensor(ms, mix_gate[:, ds(GW * g + NT, GW), :], my, ALU.mult).then_inc(sem("mixed_c"), 1)
                ve.wait_ge(sem("mixed_c"), g + 1)
                t = mix_gate[:, ds(GW * g, GW), :]
                V.tensor_tensor(t, t, ms, ALU.add).then_inc(sem("merged"), 1)
                ve.wait_ge(sem("merged_hi"), g + 1)
                low_of(hn[:, ds(GW * g, GW), META + T:META + 2 * T], t, hn[:, ds(GW * g, GW), META:META + T],
                       sem("merged_split"))

            run("branch_c", branch_c)

            def residual(base, n=None):
                def f(ph, i, s):
                    g = 2 * i + s
                    total(ph, i, s, ysum, unused=(sem("h_added"), 1 + base + g))
                    totalled(ph, i, s)
                    t = h[:, ds(GW * g, GW), :]
                    V.tensor_tensor(t, t, ysum, ALU.add).then_inc(sem("h_added"), 1)
                    if n is not None:
                        reduce_quarter(n, g)
                return f

            run("out1", residual(0, 1))
            norm(1, "norm_ffn_g", split_at=1)
            for s in range(2):
                V.memset(up_pad[s][:, :, 0:2], 0.0).then_inc(sem("up_cleared"), 1)
            ve.wait_ge(sem("up_cleared"), 2)

            def up(first, base, tiles=GW):
                def f(ph, i, s):
                    b = base + i
                    total(ph, i, s, up_pad[s][:, 0:tiles, 2:2 + T], tiles)
                    totalled(ph, i, s)
                    ve.wait_ge(sem("ff_tap"), 2 * b + s + 1)
                    for k in (1, 0):
                        for m in range(tiles):
                            t = s * FF_TILES + first + GW * i + m
                            last = V.scalar_tensor_tensor(up_conv[s][:, m, :], up_pad[s][:, m, k:k + T],
                                                          dcol(f"ffn_w{k}", t), up_conv[s][:, m, :], ALU.mult, ALU.add)
                        if k:
                            last.then_inc(sem("ff_conv_step"), 1)
                            ve.wait_ge(sem("ff_conv_step"), 2 * b + s + 1)
                    last.then_inc(sem("ff_conv"), 1)
                    if s == 0:
                        return
                    ve.wait_ge(sem("ff_conv"), 2 * b + 2)
                    ve.wait_ge(sem("ff_sigmoid"), b + 1)
                    V.tensor_tensor(ysum[:, 0:tiles, :], up_conv[0][:, 0:tiles, :], ysum[:, 0:tiles, :], ALU.mult)\
                        .then_inc(sem("ff_silu"), 1)
                    ve.wait_ge(sem("ff_silu"), b + 1)
                    ve.wait_ge(sem("ff_split"), 1 + b)
                    V.tensor_tensor(normed[0][:, 0:tiles, :], ysum[:, 0:tiles, :], up_conv[1][:, 0:tiles, :], ALU.mult)\
                        .then_inc(sem("ff_made"), 1)
                    ve.wait_ge(sem("ff_hi"), b + 1)
                    dst = act[:, ds(first % 16 + GW * i, tiles), :]
                    low_of(dst[:, :, T:2 * T], normed[0][:, 0:tiles, :], dst[:, :, 0:T], sem("ff_split"))
                return f

            run("up_0", up(0, 0))
            run("down_0", residual(4))
            run("up_1", up(16, 4))
            run("down_1", residual(8))
            run("up_2", up(32, 8))
            run("up_3", up(40, 10, 3))
            run("down_2", residual(12, 2))
            norm(2, "norm_out_g", in_place=sem("block_out"))
            for q in range(4):
                reduce_quarter(3, q)
            V.tensor_copy(lo2[:, :, 0:META], meta_lo[:, :, :].bitcast(F32)).then_inc(sem("lo2_made"), 1)
            ve.wait_ge(sem("block_out"), 4)
            norm(3, "norm1_g_2", split_at=2, wide=True)

            V.memset(lru_pad[:, :, 0:3], 0.0).then_inc(sem("lru_cleared"), 1)

            def copy_wide(dst):
                def f(ph, i, s):
                    g = 2 * i + s
                    ve.wait_ge(half_used, 1 + 2 * ph.c0 + HB(ph) * i + (s + 1) * (HB(ph) // 2))
                    V.tensor_copy(dst(g), psum[:, 4 * s:4 * s + 4, 0:TM]).then_inc(psum_freed, 1)
                return f

            run("lru_in", copy_wide(lambda g: lru_pad[:, ds(GW * g, GW), 3:3 + TM]))
            totalled(PH["lru_in"], 1, 1)
            ve.wait_ge(sem("lru_cleared"), 1)
            for q in range(4):
                ve.wait_ge(sem("lru_tap"), 4 * q + 4)
                for k in (2, 1, 0):
                    for m in range(GW):
                        f = 4 * q + m
                        last = V.scalar_tensor_tensor(xc[:, f, :], lru_pad[:, f, k:k + TM], col("conv_w_2", NT * k + f),
                                                      xc[:, f, :], ALU.mult, ALU.add)
                        if k == 0:
                            last.then_inc(sem("xc_made"), 1)
                    if k:
                        link(last)

            def xc_low(q):
                ve.wait_ge(sem("xc_hi"), q + 1)
                x = xc_parts[q % 2]
                low_of(x[:, :, TM:2 * TM], xc[:, 4 * q:4 * q + 4, :], x[:, :, 0:TM], sem("xc_split"))

            xc_low(0)
            xc_low(1)
            ve.wait_ge(sem("xc_made"), NT)
            run("pool_in", copy_wide(lambda g: pool_v[:, ds(GW * g, GW), :]))

            ph = PH["lru_gates"]
            for q in range(4):
                for s in range(2):
                    splits(ph, q, s)
                x = xc[:, 4 * q:4 * q + 4, :]
                ve.wait_ge(sem("gate_sigmoid"), 2 * q + 1)
                for m in range(GW):
                    last = V.tensor_scalar(z_q[:, m, :], z_q[:, m, :], sp8[:, 4 * q + m:4 * q + m + 1], None, ALU.mult)
                last.then_inc(psum_freed, 1)
                totalled(ph, q, 0)
                ve.sem_inc(sem("log_a_made"), 1)
                ve.wait_ge(sem("gate_sigmoid"), 2 * q + 2)
                V.tensor_tensor(x, x, i_q, ALU.mult).then_inc(psum_freed, 1)
                if q + 2 < 4:
                    xc_low(q + 2)
                totalled(ph, q, 1)
                ve.wait_ge(sem("log_a_squared"), q + 1)
                link(V.tensor_scalar(i_q, w_q, 1.0 / 42, 1.0, ALU.mult, ALU.add))
                link(V.tensor_tensor(i_q, i_q, w_q, ALU.mult))
                link(V.tensor_scalar(i_q, i_q, 1.0 / 20, 1.0, ALU.mult, ALU.add))
                link(V.tensor_tensor(i_q, i_q, w_q, ALU.mult))
                link(V.tensor_scalar(i_q, i_q, 1.0 / 6, 1.0, ALU.mult, ALU.add))
                ve.wait_ge(sem("a_made"), q + 1)
                link(V.scalar_tensor_tensor(w_q, z_q, -2.0, a_q, ALU.mult, ALU.mult))
                link(V.tensor_tensor(i_q, i_q, w_q, ALU.mult))
                link(V.tensor_tensor(w_q, a_q, a_q, ALU.mult))
                link(V.tensor_scalar(w_q, w_q, -1.0, 1.0, ALU.mult, ALU.add))
                link(V.tensor_scalar(z_q, z_q, -0.5, None, ALU.is_gt))
                link(V.copy_predicated(w_q, z_q.bitcast(mybir.dt.uint32), i_q))
                V.tensor_scalar(w_q, w_q, 1e-30, None, ALU.max).then_inc(sem("one_minus_a2"), 1)
                ve.wait_ge(sem("mult_made"), q + 1)
                link(V.tensor_tensor(x, x, w_q, ALU.mult))
                for m in range(GW):
                    t = xc[:, 4 * q + m, :]
                    last = V.tensor_tensor_scan(t, a_q[:, m, :], t, 0.0, ALU.mult, ALU.add)
                last.then_inc(sem("lru_scanned"), 1)

            t1, t2 = z_q, i_q
            ve.wait_ge(sem("lru_scanned"), 4)
            for g in range(4):
                v = pool_v[:, 4 * g:4 * g + 4, :]
                src, w = v, 1
                bufs = [t1, t2, t1, t2]
                for lvl in range(g + 1):
                    dst = bufs[lvl]
                    link(V.tensor_tensor(dst[:, :, 2 * w - 1:TM], src[:, :, 2 * w - 1:TM], src[:, :, w - 1:TM - w], ALU.add))
                    src, w = dst, 2 * w
                V.scalar_tensor_tensor(v[:, :, META:TM], src[:, :, META:TM], 1.0 / w, v[:, :, META:TM],
                                       ALU.mult, ALU.subtract).then_inc(sem("pool_diff"), 1)
                ve.wait_ge(sem("pool_hi"), g + 1)
                low_of(act[:, 4 * g:4 * g + 4, T:2 * T], v[:, :, META:TM], act[:, 4 * g:4 * g + 4, 0:T], sem("pool_split"))

            def gelu(ph, i, s):
                g = 2 * i + s
                total(ph, i, s, my, unused=(sem("lru_out"), 1 + g))
                totalled(ph, i, s)
                ve.wait_ge(sem("gelu_square"), g + 1)
                V.tensor_scalar(ms, ms, 0.044715, 1.0, ALU.mult, ALU.add).then_inc(sem("gelu_inner"), 1)
                ve.wait_ge(sem("gelu_inner"), 2 * g + 1)
                V.tensor_tensor(ms, ms, my, ALU.mult).then_inc(sem("gelu_inner"), 1)
                ve.wait_ge(sem("gelu_sigmoid"), g + 1)
                V.tensor_tensor(ms, ms, my, ALU.mult).then_inc(sem("gelu_made"), 1)
                ve.wait_ge(sem("gelu_made"), g + 1)
                t = xc[:, ds(GW * g, GW), META:TM]
                V.tensor_tensor(t, t, ms, ALU.mult).then_inc(sem("lru_out"), 1)

            run("gelu", gelu)

            def pool_mix(ph, i, s):
                g = 2 * i + s
                ve.wait_ge(sem("lru_out"), 1 + 4)
                total(ph, i, s, my, unused=(sem("pool_out"), g))
                totalled(ph, i, s)
                for m in range(GW):
                    last = V.tensor_scalar(pool_v[:, 4 * g + m, META:TM], my[:, m, :], col("pool_scale_2", 4 * g + m),
                                           None, ALU.mult)
                last.then_inc(sem("pool_out"), 1)

            run("pool_mix", pool_mix)

            def pool_gate(ph, i, s):
                g = 2 * i + s
                total(ph, i, s, my, unused=(sem("pool_out"), 4))
                ve.wait_ge(sem("pool_gate_sigmoid"), g + 1)
                t = pool_v[:, ds(GW * g, GW), META:TM]
                V.tensor_tensor(t, t, ms, ALU.mult).then_inc(sem("pool_gated"), 1)

            run("pool_gate", pool_gate)

            def lru_gate(ph, i, s):
                total(ph, i, s, my)
                g = 2 * i + s
                ve.wait_ge(sem("lru_gate_sigmoid"), g + 1)
                ve.wait_ge(sem("lru_out"), 1 + 4)
                V.tensor_tensor(mt, xc[:, ds(GW * g, GW), META:TM], ms, ALU.mult).then_inc(sem("lru_gated"), 1)
                ve.wait_ge(sem("lru_gated"), g + 1)
                ve.wait_ge(sem("pool_gated"), 4)
                t = pool_v[:, ds(GW * g, GW), META:TM]
                V.tensor_tensor(t, t, mt, ALU.add).then_inc(sem("merged2"), 1)
                ve.wait_ge(sem("merged2_hi"), g + 1)
                dst = act[:, ds(GW * g, GW), :]
                low_of(dst[:, :, T:2 * T], t, dst[:, :, 0:T], sem("merged2_split"))

            run("lru_gate", lru_gate)
            run("out2", residual(16, 4))
            norm(4, "norm2_g_2", split_at=3)

            def mlp(base):
                def f(ph, i, s):
                    g = 2 * i + s
                    total(ph, i, s, ysum, unused=(sem("h_added"), 1 + 20 + base))
                    totalled(ph, i, s)
                    ve.wait_ge(sem("mlp_split"), 1 + base + g)
                    V.scalar_tensor_tensor(normed[0], ysum, 0.0, ysum, ALU.max, ALU.mult).then_inc(sem("mlp_made"), 1)
                    ve.wait_ge(sem("mlp_hi"), base + g + 1)
                    dst = act[:, ds(GW * g, GW), :]
                    low_of(dst[:, :, T:2 * T], normed[0], dst[:, :, 0:T], sem("mlp_split"))
                return f

            for q in range(4):
                run(f"mlp1_{q}", mlp(4 * q))
                run(f"mlp2_{q}", residual(20 + 4 * q, 5 if q == 3 else None))
            norm(5, "final_g_2", in_place=sem("final_made"))


_INS = ["x", "norm_mix_g", "w_in", "b_in", "mlstm_head_g", "w_branch_m", "conv_w", "w_branch_c", "w_out",
        "norm_ffn_g", "w_up", "ffn_conv_w", "ffn_conv_b", "w_down", "norm_out_g", "meta_tokens_2",
        "norm1_g_2", "w_in_2", "pool_w_2", "pool_scale_2", "conv_w_2", "conv_b_2", "gate_a_w_2",
        "gate_a_b_2", "gate_x_w_2", "gate_x_b_2", "lru_lambda_2", "w_out_2", "norm2_g_2", "mlp_w1_2",
        "mlp_w2_2", "final_g_2"]


def kernel(**inputs):
    import numpy as np
    import concourse.bacc as bacc
    from concourse.bass_utils import run_bass_kernel_spmd

    nc = bacc.Bacc("TRN2", target_bir_lowering=False, num_devices=1)
    arrays, args = {}, {}
    for name in _INS:
        array = np.ascontiguousarray(inputs[name])
        arrays[f"in_{name}"] = array
        args[name] = nc.dram_tensor(f"in_{name}", array.shape, mybir.dt.from_np(array.dtype),
                                    kind="ExternalInput").ap()
    out = nc.dram_tensor("out", (1, T, D), F32, kind="ExternalOutput").ap()
    build(nc, args, out)
    result = run_bass_kernel_spmd(nc, [arrays], core_ids=[0])
    return result.results[0]["out"]
```

```python
import concourse.bass as bass
from concourse import mybir
from contextlib import ExitStack

F32 = mybir.dt.float32
F32R = mybir.dt.float32r
ALU = mybir.AluOpType
ACT = mybir.ActivationFunctionType
AX = mybir.AxisListType
ds = bass.ds

P = 128
D = 2048
T = 256
NT = D // P
META = 16
TM = META + T
GW = 4
CK = 4
NC = GW * P
HALF = CK // 2 * NC
RAW = 4
SLOTS = 4
AHEAD = 3
HEADS, DQK, DV = 4, 128, 256
GATE_COL = 3072
FF_TILES = 43
FF2_TILES = 64
LRU_TILES = NT
EPS = 1e-6
NEG = -1e30


class Phase:

    def __init__(self, name, groups, chunks, unroll=False):
        self.name, self.groups, self.chunks, self.unroll = name, groups, chunks, unroll
        self.bodies = groups // 2


def plan():
    names = [
        ("qkvo", 6, 4), ("conv_in", 6, 4), ("mix_gate", 8, 4),
        ("branch_m", 4, 2), ("branch_c", 4, 2), ("out1", 4, 4),
        ("up_0", 8, 4), ("down_0", 4, 4), ("up_1", 8, 4), ("down_1", 4, 4),
        ("up_2", 4, 4), ("up_3", 2, 4), ("down_2", 4, 3),
        ("lru_in", 4, 4), ("pool_in", 4, 4), ("lru_gates", 8, 0.5), ("gelu", 4, 4),
        ("pool_mix", 4, 1), ("pool_gate", 4, 4), ("lru_gate", 4, 4), ("out2", 4, 4),
    ]
    for q in range(4):
        names += [(f"mlp1_{q}", 4, 4), (f"mlp2_{q}", 4, 4)]
    unrolled = ("down_2", "pool_mix", "lru_gates", "pool_in", "up_3")
    phases, g, c = {}, 0, 0
    for name, groups, chunks in names:
        ph = Phase(name, groups, chunks, name in unrolled)
        ph.g0, ph.c0 = g, c
        g += groups
        c += int(groups * chunks)
        assert g % 2 == 0 and c % RAW == 0
        phases[name] = ph
    return phases, g, c


STAGES = [
    [("norm_mix_g", 16), ("b_in_a", 24), ("b_in_b", 56), ("mlstm_head_g", 8), ("norm_ffn_g", 16)],
    [("ffn_conv_b", 86), ("conv_w", 24), ("norm_out_g", 16)],
    [("ffn_w0", 86), ("norm1_g_2", 16), ("pool_scale_2", 16)],
    [("ffn_w1", 86), ("conv_b_2", 16), ("norm2_g_2", 16)],
    [("ffn_w2", 86), ("lru_lambda_2", 16), ("final_g_2", 16)],
    [("conv_w_2", 64), ("gate_a_b_2", 16), ("gate_x_b_2", 16)],
]
COLUMN = {}
for _s, _rows in enumerate(STAGES):
    _at = 0
    for _name, _n in _rows:
        COLUMN[_name] = (_s * P + _at, _n)
        _at += _n


def build(nc, a, out):
    PH, GROUPS, CHUNKS = plan()
    ctx = ExitStack()
    with ctx:
        def sb(name, shape, dt=F32, stack=ctx):
            return stack.enter_context(nc.sbuf_tensor(name, shape, dt))

        sems = {}

        def sem(name):
            if name not in sems:
                sems[name] = ctx.enter_context(nc.semaphore(name))
            return sems[name]

        raw = sb("raw", [P, RAW, CK * NC])
        whi = sb("whi", [P, SLOTS, HALF], F32R)
        wlo = sb("wlo", [P, SLOTS, HALF], F32R)
        h = sb("h", [P, NT, T])
        hn = sb("hn", [P, NT, META + 2 * T], F32R)
        act = sb("act", [P, NT, 2 * T], F32R)
        meta_lo = sb("meta_lo", [P, NT, META], F32R)
        lowc = sb("lowc", [P, GW, T])
        cols = sb("cols", [P, len(STAGES) * P])
        ident = sb("ident", [P, P])
        ones = sb("ones", [P, T])
        eps = sb("eps", [P, 1])
        tiny = sb("tiny", [P, 1])
        scale = sb("scale", [P, TM])
        gain2 = sb("gain2", [P, NT])
        rms_out = sb("rms_out", [P, 2])
        sp8 = sb("sp8", [P, NT])
        work = sb("work", [P, 8752])
        with ExitStack() as early:
            lo2 = sb("lo2", [P, NT, TM], F32R, early)
        misc = sb("misc", [P, NT * TM])

        psum = ctx.enter_context(nc.psum_tensor("psum", [P, 8, 512], F32))

        def view(t, at, *shape):
            n = 1
            for s in shape:
                n *= s
            v = t[:, at:at + n]
            if len(shape) == 2:
                v = v.rearrange("p (a b) -> p a b", b=shape[1])
            return v

        def col(name, i=0):
            return cols[:, COLUMN[name][0] + i:COLUMN[name][0] + i + 1]

        def dcol(name, i):
            return cols[:, ds(COLUMN[name][0] + i, 1)]

        ysum = view(work, 4112, GW, T)
        made = view(work, 5136, GW, T)
        squares = view(work, 6160, GW, T)
        part = view(work, 7184, 4, T)
        squares2, part2 = view(work, 0, GW, T), view(work, 1024, 4, T)
        r1, r2 = work[:, 8208:8208 + T], work[:, 8464:8464 + T]
        stream_scale = scale[:, META:TM]

        def over_tiles(row, n=GW):
            return row.unsqueeze(1).to_broadcast([P, n, row.shape[1]])
        my = view(misc, 0, GW, T)
        ms = view(misc, 1024, GW, T)
        mt = view(misc, 2048, GW, T)
        x_nat = view(work, 0, 2, D)
        meta_nat = misc[0:META, 0:D]
        meta_sq = misc[0:META, D:2 * D]
        meta_ss = misc[0:META, 2 * D:2 * D + 2]
        stage = view(work, 4112, len(STAGES), P)
        wif = view(work, 8208, NT, 8)
        qkvo = view(work, 0, 24, T)
        v_tok = view(work, 6144, 2, HEADS * DV)
        conv_in = view(work, 0, 24, T)
        conv_pad = view(work, 6144, 8, T + 2)
        mix_gate = view(work, 0, 32, T)
        up_pad = [view(work, 0, GW, T + 2), view(work, 1032, GW, T + 2)]
        up_conv = [view(work, 2064, GW, T), view(work, 3088, GW, T)]
        lru_pad = view(work, 0, NT, TM + 3)
        pool_v = view(work, 0, NT, TM)
        xc = view(work, 4400, NT, TM)
        out_nat = view(work, 0, 2, D)
        act_flat = act[:, :, :].rearrange("p a b -> p (a b)")
        xc_parts = [view(act_flat, j * GW * 2 * TM, GW, 2 * TM) for j in range(2)]
        row_a, row_b, row_c, row_guard = [lowc[0:HEADS, j, :] for j in range(4)]
        logits = misc[0:2 * HEADS, 4096:4352]
        decay = view(misc, 0, HEADS, T + P)
        scores = view(misc, 1536, HEADS, T + P)
        num_sq = [view(misc, 3072 + 512 * j, 2, T) for j in range(2)]
        factor = view(misc, 0, HEADS, T)
        ccol = sb("ccol", [P, 2, HEADS])
        gate_b = sb("gate_b", [2 * HEADS, 1])
        z_q, i_q, a_q, w_q = [view(misc, j * GW * TM, GW, TM) for j in range(4)]
        lam = [view(work, 8592 + NT * j, 1, NT).rearrange("p a b -> p (a b)") for j in range(4)]

        mask = work[:, 8336:8336 + T]
        onecol = sb("onecol", [P, HEADS, HEADS])

        chunk_loaded = [sem(f"chunk_loaded_{r}") for r in range(RAW)]
        hi_ready, lo_ready, half_used = sem("hi_ready"), sem("lo_ready"), sem("half_used")
        low_copied, psum_freed = sem("low_copied"), sem("psum_freed")
        STARTS_AT_ONE = ("h_added", "mixed_m", "merged", "lru_out", "ff_split", "mlp_split")
        C_GATES = PH["lru_gates"].c0

        NO_LOW = ("lru_in", "pool_in", "lru_gates")
        n = 0
        for ph in PH.values():
            ph.lc0 = n
            if ph.name not in NO_LOW:
                n += ph.groups

        SCALED = ("qkvo", "conv_in", "mix_gate", "up_0", "up_1", "up_2", "up_3", "gelu", "pool_gate", "lru_gate",
                  "mlp1_0", "mlp1_1", "mlp1_2", "mlp1_3")
        n = 0
        for ph in PH.values():
            ph.sc0 = n
            if ph.name in SCALED:
                n += ph.groups
        for ph in PH.values():
            ph.scale = 1 + (ph.g0 >= PH["up_0"].g0) + (ph.g0 >= PH["lru_in"].g0) + (ph.g0 >= PH["mlp1_0"].g0)

        def by_tiles(w):
            return w.rearrange("(k p) n -> p k n", p=P)

        W_in, W_in2 = by_tiles(a["w_in"]), by_tiles(a["w_in_2"][0])
        W_bm, W_bc = by_tiles(a["w_branch_m"]), by_tiles(a["w_branch_c"])
        W_o, W_o2 = by_tiles(a["w_out"]), by_tiles(a["w_out_2"][0])
        W_up, W_down = by_tiles(a["w_up"]), by_tiles(a["w_down"])
        W_m1, W_m2 = by_tiles(a["mlp_w1_2"][0]), by_tiles(a["mlp_w2_2"][0])
        W_pool = [by_tiles(a["pool_w_2"][0, g]) for g in range(4)]
        W_ga = a["gate_a_w_2"][0].rearrange("h (k p) n -> p (h k) n", p=P)
        W_gx = a["gate_x_w_2"][0].rearrange("h (k p) n -> p (h k) n", p=P)

        SOURCE = {
            "qkvo": (W_in, 0, 0), "conv_in": (W_in, 0, 3080), "mix_gate": (W_in, 0, 6152),
            "branch_m": (W_bm, 0, 0), "branch_c": (W_bc, 0, 0), "out1": (W_o, 0, 0),
            "down_0": (W_down, 0, 0), "down_1": (W_down, 16, 0), "down_2": (W_down, 32, 0),
            "lru_in": (W_in2, 0, D), "pool_in": (W_in2, 0, 0), "gelu": (W_in2, 0, 2 * D),
            "pool_gate": (W_in2, 0, 3 * D), "lru_gate": (W_in2, 0, 4 * D), "out2": (W_o2, 0, 0),
        }
        for q in range(4):
            SOURCE[f"mlp1_{q}"] = (W_m1, 0, q * D)
            SOURCE[f"mlp2_{q}"] = (W_m2, q * NT, 0)
        UP_FIRST = {"up_0": 0, "up_1": 16, "up_2": 32, "up_3": 40}

        block = ctx.enter_context(nc.Block())

        def HB(ph):
            return int(4 * ph.chunks)

        def chunk_value(ph, i, loc):
            if isinstance(i, int):
                half = 2 * ph.c0 + HB(ph) * i + loc
                return 16 * (half // 2 // RAW + 1) + (16 if half // 2 >= C_GATES else 0)
            first = ph.c0 // RAW + (HB(ph) // 2 // RAW) * i
            return 16 * (first + loc // 2 // RAW + 1) + (16 if ph.c0 >= C_GATES else 0)

        def last_of_all(ph, i, loc):
            return 2 * ph.c0 + HB(ph) * i + loc >= 2 * CHUNKS

        def half_number(ph, i, loc):
            return 2 * ph.c0 + HB(ph) * i + loc if isinstance(i, int) else loc

        def nothing(j, ph, i, s):
            pass

        def follow(left, j):
            step, ph, i, s = left
            step(j, ph, i, s)

        def stream(eng, ph, split, step, left, first=None, final=None):
            n = HB(ph) // 2
            end = ph.bodies - 1

            def body(i, left, first, at_end):
                for s in range(2):
                    for k in range(n):
                        if not isinstance(i, int) or not last_of_all(ph, i, AHEAD + s * n + k):
                            split(ph, i, AHEAD + s * n + k)
                        if first:
                            first(s * n + k)
                        for j in (k + 1,) if k < n - 1 else range(n, STEPS):
                            follow(left, j)
                    left = (final if final and at_end and s == 1 else step, ph, i, s)
                    follow(left, 0)
                return left

            left = body(0, left, first, end == 0)
            if end > 2:
                with eng.Fori(1, end) as i:
                    body(i, (step, ph, i - 1, 1), None, False)
                left = (step, ph, end - 1, 1)
            elif end == 2:
                left = body(1, left, None, False)
            if end:
                left = body(end, left, None, True)
            return left

        def finish(left):
            for j in range(1, STEPS):
                follow(left, j)
            return (nothing, None, 0, 0)

        STAGE_DMAS = sum(len(r) for r in STAGES)
        STEPS = 8
        MIDDLE = 3
        NORM_SQUARES = {0: 4, 1: 8, 2: 16, 3: 20, 4: 24}

        @block.sync
        def _(sp):
            def load_x(q):
                sp.dma_start(x_nat[:, :, q * 512:(q + 1) * 512],
                             a["x"][0].rearrange("(t p) n -> p t n", p=P)[:, :, q * 512:(q + 1) * 512])\
                    .then_inc(sem(f"x_loaded_{q}"), 16)

            def load(c, c_slot, dst_cols, src):
                if not (isinstance(c, int) and c < RAW):
                    sp.wait_ge(lo_ready, 2 * c - 2 * RAW + 2)
                kt, n = src.shape[1], src.shape[2]
                dst = raw[:, c_slot % RAW, :].rearrange("p (k n) -> p k n", n=dst_cols)[:, 0:kt, 0:n]
                sp.dma_start(dst, src).then_inc(chunk_loaded[c_slot % RAW], 16)

            def load_group(ph, body, i, s):
                nch = ph.chunks
                per_body = 2 * nch
                if ph.name.startswith("up"):
                    tiles = 3 if ph.name == "up_3" else GW
                    first = UP_FIRST[ph.name] * P + s * FF_TILES * P
                    w, k0, c_first = W_up, 0, first
                    column, n = c_first + i * NC, tiles * P
                else:
                    w, k0, c_first = SOURCE[ph.name]
                    column, n = c_first + (2 * i + s) * NC, NC
                for j in range(nch):
                    if ph.name == "qkvo" and body == 0 and s == 0:
                        load_x(j)
                    kt = min(CK, w.shape[1] - k0 - CK * j)
                    cl = s * nch + j
                    load(ph.c0 + per_body * i + cl, cl + (body * per_body if ph.unroll else 0), NC,
                         w[:, k0 + CK * j:k0 + CK * j + kt, ds(column, n)])

            for ph in PH.values():
                if ph.name == "lru_gates":
                    for q in range(4):
                        sp.wait_ge(lo_ready, 2 * (ph.c0 + q) - 2 * RAW + 2)
                        for s, w in enumerate((W_ga, W_gx)):
                            sp.dma_start(raw[:, q, s * HALF:(s + 1) * HALF].rearrange("p (k n) -> p k n", n=256),
                                         w[:, 4 * q:4 * q + 4, :]).then_inc(chunk_loaded[q], 16)
                elif ph.name == "pool_mix":
                    for g in range(4):
                        load(ph.c0 + g, g, NC, W_pool[g])
                elif ph.unroll or ph.name == "qkvo":
                    for i in range(ph.bodies):
                        for s in range(2):
                            load_group(ph, i, i, s)
                else:
                    with sp.Fori(0, ph.bodies) as i:
                        for s in range(2):
                            load_group(ph, 0, i, s)

            for t in range(2):
                for half in range(2):
                    c = slice(half * D // 2, (half + 1) * D // 2)
                    for e in ("even", "odd"):
                        sp.wait_ge(sem(f"out_copied_{e}"), 2 * t + half + 1)
                    sp.dma_start(out[0, t * P:(t + 1) * P, c], out_nat[:, t, c]).then_inc(sem("out_stored"), 16)
            sp.wait_ge(sem("out_stored"), 64)

        @block.gpsimd
        def _(pool):
            pool.memset(ident[:, :], 0.0).then_inc(sem("const_cleared"), 1)
            pool.memset(mask, 0.0).then_inc(sem("const_cleared"), 1)
            pool.memset(onecol[:, :, :], 0.0).then_inc(sem("const_cleared"), 1)
            pool.memset(ones[:, :], 1.0).then_inc(sem("ones_ready"), 1)
            pool.memset(eps[:, :], EPS).then_inc(sem("ones_ready"), 1)
            pool.memset(tiny[:, :], 1e-30).then_inc(sem("ones_ready"), 1)
            pool.memset(scale[:, 0:META], 1.0).then_inc(sem("ones_ready"), 1)
            pool.wait_ge(sem("const_cleared"), 3)
            pool.affine_select(out=ident[:, :], in_=ident[:, :], compare_op=ALU.not_equal, fill=1.0,
                               base=0, pattern=[[-1, P]], channel_multiplier=1).then_inc(sem("consts_ready"), 1)
            pool.affine_select(out=mask, in_=mask, compare_op=ALU.is_ge, fill=NEG,
                               base=0, pattern=[[1, T]], channel_multiplier=-1).then_inc(sem("consts_ready"), 1)
            pool.affine_select(out=onecol[:, :, :], in_=onecol[:, :, :], compare_op=ALU.not_equal, fill=1.0,
                               base=0, pattern=[[1, HEADS], [-1, HEADS]], channel_multiplier=0).then_inc(sem("consts_ready"), 1)

        @block.tensor
        def _(pe):
            mm = nc.tensor.matmul
            pe.sem_inc(half_used, 1)

            def spread_row(hd):
                return ident[0:HEADS, hd:hd + 1].to_broadcast([HEADS, P])

            def turn_x(b):
                pe.wait_ge(sem(f"x_loaded_{b // 2}"), 16)
                for f in range(2):
                    for t in range(2):
                        last = nc.tensor.transpose(psum[:, b, f * T + t * P:f * T + (t + 1) * P],
                                                   x_nat[:, t, (2 * b + f) * P:(2 * b + f + 1) * P], ident[:, :])
                last.then_inc(sem("x_turned"), 1)

            pe.wait_ge(sem("consts_ready"), 3)
            for b in range(4):
                turn_x(b)
            pe.wait_ge(sem("stage_loaded"), STAGE_DMAS * 16)
            for s, rows in enumerate(STAGES):
                nr = sum(n for _, n in rows)
                last = nc.tensor.transpose(psum[:, 4 + s // 4, (s % 4) * P:(s % 4) * P + nr],
                                           stage[0:nr, s, :], ident[0:nr, 0:nr])
            last.then_inc(sem("cols_turned"), 1)
            for b in range(4, 8):
                if b in (4, 5):
                    pe.wait_ge(sem("cols_copied"), b - 3)
                turn_x(b)

            def norm_total(n, rows=1):
                pe.wait_ge(sem("squares_summed"), NORM_SQUARES[n])
                for src in range(rows):
                    for q in range(4):
                        last = mm(psum[:, 4, src * T:(src + 1) * T], ones[:, 0:P], (part, part2)[src][:, q, :],
                                  start=(q == 0), stop=(q == 3))
                last.then_inc(sem("norm_total"), 1)

            def group(ph, i, s, body, rhs, kts, tiles=GW, waits=(), middle=None):
                g = ph.g0 + 2 * i + s
                pe.wait_ge(psum_freed, g + 1)
                nh = int(2 * ph.chunks)
                for k in range(nh):
                    if k % 2 == 0 and k // 2 < len(waits):
                        pe.wait_ge(*waits[k // 2])
                    hl = s * nh + k + (body * 2 * nh)
                    pe.wait_ge(lo_ready, 2 * ph.c0 + (2 * nh) * i + s * nh + k + 1)
                    hi = whi[:, hl % SLOTS, :].rearrange("p (k n) -> p k n", n=NC)
                    lo = wlo[:, hl % SLOTS, :].rearrange("p (k n) -> p k n", n=NC)
                    for kk in range(2):
                        kt = 2 * k + kk
                        if kt >= kts:
                            continue
                        both = rhs(kt)
                        first, end = kt == 0, kt == kts - 1
                        for m in range(tiles):
                            o = psum[:, 4 * s + m, :]
                            wide = lambda: mm(o, hi[:, kk, m * P:(m + 1) * P], both, start=first, stop=end)
                            narrow = lambda: mm(o[:, 0:T], lo[:, kk, m * P:(m + 1) * P], both[:, 0:T],
                                                start=False, stop=False)
                            if first:
                                wide()
                                last = narrow()
                            else:
                                narrow()
                                last = wide()
                    last.then_inc(half_used, 1)
                    if middle and k == MIDDLE:
                        middle()

            def group_wide(ph, i, s, body, waits=(), middle=None):
                g = ph.g0 + 2 * i + s
                pe.wait_ge(psum_freed, g + 1)
                nh = int(2 * ph.chunks)
                for k in range(nh):
                    if k % 2 == 0 and k // 2 < len(waits):
                        pe.wait_ge(*waits[k // 2])
                    hl = s * nh + k + (body * 2 * nh)
                    pe.wait_ge(lo_ready, 2 * ph.c0 + (2 * nh) * i + s * nh + k + 1)
                    hi = whi[:, hl % SLOTS, :].rearrange("p (k n) -> p k n", n=NC)
                    lo = wlo[:, hl % SLOTS, :].rearrange("p (k n) -> p k n", n=NC)
                    for kk in range(2):
                        kt = 2 * k + kk
                        for m in range(GW):
                            o = psum[:, 4 * s + m, 0:TM]
                            w = slice(m * P, (m + 1) * P)
                            mm(o, hi[:, kk, w], hn[:, kt, 0:TM], start=(kt == 0), stop=False)
                            mm(o, hi[:, kk, w], lo2[:, kt, :], start=False, stop=False)
                            last = mm(o, lo[:, kk, w], hn[:, kt, 0:TM], start=False, stop=(kt == NT - 1))
                    last.then_inc(half_used, 1)
                    if middle and k == MIDDLE:
                        middle()

            def run(name, rhs, kts=NT, tiles=(GW, GW), waits=(), middle=None, freed=None):
                ph = PH[name]

                def body(i, number, first):
                    for s in range(2):
                        if first and s == 1 and freed:
                            pe.wait_ge(*freed)
                        m = middle if first and s == 0 else None
                        w = waits if first and s == 0 else ()
                        if rhs is None:
                            group_wide(ph, i, s, number, w, m)
                        else:
                            group(ph, i, s, number, rhs, kts, tiles[s], w, m)

                start = 0
                if ph.unroll or middle or waits:
                    body(0, 0, True)
                    start = 1
                if ph.unroll:
                    for i in range(1, ph.bodies):
                        body(i, i, False)
                elif ph.bodies - start == 1:
                    body(start, 0, False)
                else:
                    with pe.Fori(start, ph.bodies) as i:
                        body(i, 0, False)

            def from_hn(kt):
                return hn[:, kt, META:META + 2 * T]

            def operand_waits(n):
                return [(sem("operand_split"), 4 * n + q + 1) for q in range(4)]

            def setup_sums():
                pe.wait_ge(psum_freed, 2)
                norm_total(0)
                pe.wait_ge(sem("meta_normed"), 1)
                for f in range(NT):
                    last = nc.tensor.transpose(psum[:, 6, f * META:(f + 1) * META],
                                               meta_nat[:, f * P:(f + 1) * P], ident[0:META, 0:META])
                last.then_inc(sem("meta_turned"), 1)
                pe.wait_ge(sem("gates_scaled"), 1)
                for kt in range(NT):
                    last = mm(psum[0:8, 7, 0:T], wif[:, kt, :], h[:, kt, :], start=(kt == 0), stop=(kt == NT - 1))
                last.then_inc(sem("if_made"), 1)

            run("qkvo", from_hn, waits=operand_waits(0), middle=setup_sums, freed=(sem("logits_made"), 1))

            pe.wait_ge(sem("biased"), 6)
            mm(psum[0:HEADS, 4, 0:T], ident[0:8, HEADS:8], logits, start=True, stop=True)\
                .then_inc(sem("f_moved"), 1)
            for t in range(2):
                for j in range(2):
                    for f in range(4):
                        last = nc.tensor.transpose(psum[:, 2 * t + j, f * P:(f + 1) * P],
                                                   qkvo[:, 8 + 4 * j + f, t * P:(t + 1) * P], ident[:, :])
                    last.then_inc(sem("v_turned"), 1)
            pe.wait_ge(sem("m_ready"), 1)
            for t in range(2):
                last = nc.tensor.transpose(psum[:, 6, t * HEADS:(t + 1) * HEADS],
                                           row_c[:, t * P:(t + 1) * P], ident[0:HEADS, 0:HEADS])
            last.then_inc(sem("c_turned"), 1)
            for hd in range(HEADS):
                last = mm(psum[:, 4 + hd // 2, hd % 2 * T:(hd % 2 + 1) * T], spread_row(hd), row_b,
                          start=True, stop=True)
            last.then_inc(sem("m_spread"), 1)

            def score(hd):
                if hd == 0:
                    pe.wait_ge(sem("z_made"), 1)
                if hd >= 2:
                    pe.wait_ge(sem("st_made"), hd - 1)
                o = psum[:, 6 + hd % 2, :]
                mm(o[:, 0:T], qkvo[:, 4 + hd, 0:P], qkvo[:, hd, :], start=True, stop=True)
                mm(o[:, T:T + P], qkvo[:, 4 + hd, P:T], qkvo[:, hd, P:T], start=True, stop=True)\
                    .then_inc(sem("scores_made"), 1)

            def squares_of(hd):
                pe.wait_ge(sem("num_squared"), hd + 1)
                for v in range(2):
                    last = mm(psum[0:HEADS, 5, 0:T], onecol[:, hd, :], num_sq[hd % 2][:, v, :],
                              start=(hd == 0 and v == 0), stop=(hd == HEADS - 1 and v == 1))
                last.then_inc(sem("squares_used"), 1)

            score(0)
            score(1)
            pe.wait_ge(sem("v_copied"), 4)
            for hd in range(HEADS):
                pe.wait_ge(sem("st_made"), hd + 1)
                for v in range(2):
                    o = psum[:, hd, v * T:(v + 1) * T]
                    c = slice(hd * DV + v * P, hd * DV + (v + 1) * P)
                    mm(o, v_tok[:, 0, c], scores[:, hd, 0:T], start=True, stop=False)
                    last = mm(o[:, P:T], v_tok[:, 1, c], scores[:, hd, T:T + P], start=False, stop=True)
                last.then_inc(sem("num_made"), 1)
                mm(psum[0:HEADS, 4, 0:T], onecol[:, hd, :], scores[:, hd, 0:T], start=(hd == 0), stop=False)
                mm(psum[0:HEADS, 4, P:T], onecol[:, hd, :], scores[:, hd, T:T + P], start=False,
                   stop=(hd == HEADS - 1)).then_inc(sem("den_made"), 1)
                if hd + 2 < HEADS:
                    score(hd + 2)
                if hd >= 1:
                    squares_of(hd - 1)
            squares_of(HEADS - 1)
            pe.wait_ge(sem("factor_made"), 1)
            for hd in range(HEADS):
                last = mm(psum[:, 6 + hd // 2, hd % 2 * T:(hd % 2 + 1) * T], spread_row(hd), row_a,
                          start=True, stop=True)
            last.then_inc(sem("factor_spread"), 1)
            pe.wait_ge(sem("hm_scaled"), 8)

            run("conv_in", from_hn)
            run("mix_gate", from_hn)
            run("branch_m", lambda kt: act[:, kt, :], kts=8, waits=[(sem("hm_split"), 1), (sem("hm_split"), 2)])
            run("branch_c", lambda kt: act[:, 8 + kt, :], kts=8, waits=[(sem("conv_split"), 1), (sem("conv_split"), 2)])
            from_act = lambda kt: act[:, kt, :]
            run("out1", from_act, waits=[(sem("merged_split"), q + 1) for q in range(4)])
            run("up_0", from_hn, waits=operand_waits(1), middle=lambda: norm_total(1), freed=(sem("norm_root"), 2))
            run("down_0", from_act, waits=[(sem("ff_split"), 1 + q + 1) for q in range(4)])
            run("up_1", from_hn)
            run("down_1", from_act, waits=[(sem("ff_split"), 1 + q + 5) for q in range(4)])
            run("up_2", from_hn)
            run("up_3", from_hn, tiles=(3, 3))
            run("down_2", from_act, kts=11, waits=[(sem("ff_split"), 1 + q + 9) for q in range(3)])

            run("lru_in", None, waits=[(sem("lo2_made"), 1 + q + 1) for q in range(4)], middle=lambda: norm_total(2, 2), freed=(sem("second_sum_used"), 1))
            run("pool_in", None)
            ph = PH["lru_gates"]
            for q in range(4):
                pe.wait_ge(sem("xc_split"), q + 1)
                xq = xc_parts[q % 2]
                for s in range(2):
                    g = ph.g0 + 2 * q + s
                    pe.wait_ge(psum_freed, g + 1)
                    H = 2 * ph.c0 + 2 * q + s
                    pe.wait_ge(lo_ready, H + 1)
                    hi = whi[:, H % SLOTS, :].rearrange("p (h k n) -> p h k n", h=2, k=2)
                    lo = wlo[:, H % SLOTS, :].rearrange("p (h k n) -> p h k n", h=2, k=2)
                    for m in range(GW):
                        o = psum[:, 4 * s + m, 0:TM]
                        w = slice(m % 2 * P, (m % 2 + 1) * P)
                        for k in range(2):
                            kt = 2 * (m // 2) + k
                            mm(o, hi[:, m // 2, k, w], xq[:, kt, 0:TM], start=(k == 0), stop=False)
                            mm(o, hi[:, m // 2, k, w], xq[:, kt, TM:2 * TM], start=False, stop=False)
                            last = mm(o, lo[:, m // 2, k, w], xq[:, kt, 0:TM], start=False, stop=(k == 1))
                    last.then_inc(half_used, 1)
            run("gelu", from_hn)
            ph = PH["pool_mix"]
            for i in range(2):
                for s in range(2):
                    g4 = 2 * i + s
                    group(ph, i, s, i, lambda kt: act[:, 4 * g4 + kt, :], 4, waits=[(sem("pool_split"), g4 + 1)])
            run("pool_gate", from_hn)
            run("lru_gate", from_hn)
            run("out2", from_act, waits=[(sem("merged2_split"), q + 1) for q in range(4)])
            for q in range(4):
                if q == 0:
                    run("mlp1_0", from_hn, waits=operand_waits(3), middle=lambda: norm_total(3),
                        freed=(sem("norm_root"), 5))
                else:
                    run(f"mlp1_{q}", from_hn)
                run(f"mlp2_{q}", from_act, waits=[(sem("mlp_split"), 1 + 4 * q + j + 1) for j in range(4)])
            pe.wait_ge(psum_freed, GROUPS + 2)
            for q in range(4):
                pe.wait_ge(sem("final_made"), q + 1)
                if q == 3:
                    pe.wait_ge(sem("squares_summed"), NORM_SQUARES[4])
                    for t in range(2):
                        for j in range(4):
                            last = mm(psum[:, 7, t:t + 1], part[:, j, t * P:(t + 1) * P], ones[:, 0:1],
                                      start=(j == 0), stop=(j == 3))
                    last.then_inc(sem("norm_total"), 1)
                for t in range(2):
                    if q == 3 and t == 1:
                        pe.wait_ge(sem("norm_root"), 6)
                    for f in range(4):
                        last = nc.tensor.transpose(psum[:, 4 * t + q, f * P:(f + 1) * P],
                                                   h[:, 4 * q + f, t * P:(t + 1) * P], ident[:, :])
                    last.then_inc(sem("out_turned"), 1)

        @block.scalar
        def _(ac):
            A = nc.scalar.activation

            def rows(src, r):
                return src.rearrange("(r p) -> r p", p=P)[0:r, :]

            source = {
                "norm_mix_g": a["norm_mix_g"], "b_in_a": a["b_in"][0:GATE_COL], "b_in_b": a["b_in"][GATE_COL + 8:],
                "mlstm_head_g": a["mlstm_head_g"], "norm_ffn_g": a["norm_ffn_g"], "ffn_conv_b": a["ffn_conv_b"],
                "norm_out_g": a["norm_out_g"], "ffn_w0": a["ffn_conv_w"][0], "ffn_w1": a["ffn_conv_w"][1],
                "ffn_w2": a["ffn_conv_w"][2], "norm1_g_2": a["norm1_g_2"][0], "pool_scale_2": a["pool_scale_2"][0],
                "conv_b_2": a["conv_b_2"][0], "norm2_g_2": a["norm2_g_2"][0], "lru_lambda_2": a["lru_lambda_2"][0],
                "final_g_2": a["final_g_2"],
                "conv_w": a["conv_w"].rearrange("k (r p) -> (k r) p", p=P),
                "conv_w_2": a["conv_w_2"][0].rearrange("k (r p) -> (k r) p", p=P),
                "gate_a_b_2": a["gate_a_b_2"][0].rearrange("h (r p) -> (h r) p", p=P),
                "gate_x_b_2": a["gate_x_b_2"][0].rearrange("h (r p) -> (h r) p", p=P),
            }
            ac.dma_start(meta_nat, a["meta_tokens_2"]).then_inc(sem("meta_loaded"), 16)
            for s, rws in enumerate(STAGES):
                at = 0
                for name, n in rws:
                    src = source[name]
                    if len(src.shape) == 1:
                        src = rows(src, n)
                    ac.dma_start(stage[at:at + n, s, :], src).then_inc(sem("stage_loaded"), 16)
                    at += n
            ac.dma_start(wif, by_tiles(a["w_in"])[:, :, GATE_COL:GATE_COL + 8]).then_inc(sem("gates_loaded"), 16)
            ac.dma_start(gate_b[:, :], a["b_in"][GATE_COL:GATE_COL + 8].rearrange("(r o) -> r o", o=1))\
                .then_inc(sem("gate_b_loaded"), 16)

            def split(ph, i, loc):
                hc = 2 * ph.c0 + HB(ph) * i + loc
                n = half_number(ph, i, loc)
                ac.wait_ge(chunk_loaded[n // 2 % RAW], chunk_value(ph, i, loc))
                if not (isinstance(hc, int) and hc < SLOTS):
                    ac.wait_ge(half_used, 1 + hc - SLOTS + 1)
                A(whi[:, n % SLOTS, :], raw[:, n // 2 % RAW, n % 2 * HALF:(n % 2 + 1) * HALF], ACT.Copy)\
                    .then_inc(hi_ready, 1)

            def low(ph, i, s, tiles=GW):
                ac.wait_ge(half_used, 1 + HB(ph) * i + 2 * ph.c0 + (s + 1) * (HB(ph) // 2))
                ac.wait_ge(psum_freed, ph.g0 + 2 * i + s + 2)
                A(lowc[:, 0:tiles, :], psum[:, 4 * s:4 * s + tiles, T:2 * T], ACT.Copy).then_inc(low_copied, 1)

            def scaled(ph, i, s):
                ac.wait_ge(sem("scaled"), ph.sc0 + 2 * i + s + 1)

            def run(name, step, left, first=None, final=None):
                return stream(ac, PH[name], split, step, left, first, final)

            def low_only(j, ph, i, s):
                if j == 0:
                    low(ph, i, s)

            def root(n):
                ac.wait_ge(sem("norm_total"), n + 1)
                A(stream_scale, psum[:, 4, 0:T], ACT.Sqrt, bias=eps[:, 0:1], scale=1.0 / D).then_inc(sem("norm_root"), 1)

            def at_norm(n):
                return lambda x: root(n) if x == MIDDLE + 1 else None

            def high(g, gain):
                for m in range(GW):
                    last = A(hn[:, ds(GW * g + m, 1), META:META + T], h[:, ds(GW * g + m, 1), :], ACT.Copy,
                             scale=gain(GW * g + m))
                last.then_inc(sem("operand_hi"), 1)

            def square(count, g, gain=None):
                ac.wait_ge(sem("squares_summed"), count)
                if gain is None:
                    A(squares, h[:, ds(GW * g, GW), :], ACT.Square).then_inc(sem("squared"), 1)
                else:
                    for m in range(GW):
                        last = A(squares2[:, m:m + 1, :], h[:, ds(GW * g + m, 1), :], ACT.Square, scale=gain(GW * g + m))
                    last.then_inc(sem("squared"), 1)

            ac.wait_ge(sem("meta_loaded"), 16)
            ac.wait_ge(sem("ones_ready"), 4)
            A(meta_sq, meta_nat, ACT.Square, accum_out=meta_ss[:, 0:1]).then_inc(sem("meta_squared"), 1)
            ac.wait_ge(sem("meta_squared"), 1)
            A(meta_ss[:, 1:2], meta_ss[:, 0:1], ACT.Sqrt, bias=eps[0:META, 0:1], scale=1.0 / D)\
                .then_inc(sem("meta_root"), 1)
            ac.wait_ge(sem("cols_copied"), 2)
            for q in range(4):
                ac.wait_ge(sem("x_copied"), 2 * q + 2)
                high(q, lambda t: col("norm_mix_g", t))
                if q < AHEAD:
                    split(PH["qkvo"], 0, q)
                square(q, q)
            c0, n0 = COLUMN["lru_lambda_2"]
            A(lam[0], cols[:, c0:c0 + n0], ACT.Abs).then_inc(sem("lam_abs"), 1)
            ac.wait_ge(sem("lam_abs"), 1)
            A(lam[0], lam[0], ACT.Exp, scale=-1.0).then_inc(sem("lam_exp"), 1)

            def add_bias(tiles, name, done, func):
                def step(j, ph, i, s):
                    if j == 0:
                        low(ph, i, s)
                    elif j == 1:
                        scaled(ph, i, s)
                        for m in range(GW):
                            f = GW * (2 * i + s) + m
                            t = tiles[:, ds(f, 1), :]
                            last = A(t, t, func(i), bias=dcol(name[0], name[1] + f))
                        last.then_inc(sem(done), 1)
                return step

            left = (nothing, None, 0, 0)
            left = run("qkvo", add_bias(qkvo, ("b_in_a", 0), "biased",
                                        lambda i: ACT.Sigmoid if isinstance(i, int) and i == 2 else ACT.Identity),
                       left, first=at_norm(0))
            left = finish(left)

            ac.wait_ge(sem("f_copied"), 1)
            A(row_a, row_c, ACT.Abs).then_inc(sem("f_step"), 1)
            ac.wait_ge(sem("f_step"), 1)
            A(row_a, row_a, ACT.Exp, scale=-1.0).then_inc(sem("f_step"), 1)
            ac.wait_ge(sem("f_step"), 2)
            A(row_a, row_a, ACT.Ln, bias=1.0).then_inc(sem("f_step"), 1)
            ac.wait_ge(sem("guard_sum"), 1)
            A(row_guard, row_guard, ACT.Exp, scale=-1.0).then_inc(sem("guard_ready"), 1)
            ac.wait_ge(sem("z_made"), 1)
            for hd in range(HEADS):
                A(decay[:, hd, 0:T], decay[:, hd, 0:T], ACT.Exp, bias=ccol[:, 0, hd:hd + 1])
                A(decay[:, hd, T:T + P], decay[:, hd, T:T + P], ACT.Exp, bias=ccol[:, 1, hd:hd + 1])\
                    .then_inc(sem("decay_made"), 1)
            for hd in range(HEADS):
                ac.wait_ge(sem("num_made"), hd + 1)
                if hd >= 2:
                    ac.wait_ge(sem("squares_used"), hd - 1)
                A(num_sq[hd % 2], psum[:, hd, :].rearrange("p (a b) -> p a b", b=T), ACT.Square)\
                    .then_inc(sem("num_squared"), 1)
            ac.wait_ge(sem("den_made"), HEADS)
            A(row_a, psum[0:HEADS, 4, 0:T], ACT.Abs).then_inc(sem("den_abs"), 1)
            ac.wait_ge(sem("ms_made"), 1)
            A(row_b, row_b, ACT.Sqrt, bias=eps[0:HEADS, 0:1], scale=1.0 / DV).then_inc(sem("ms_root"), 1)
            ac.wait_ge(sem("factor_spread"), 1)
            A(factor, psum[:, 6:8, :].rearrange("p a (b t) -> p (a b) t", t=T), ACT.Copy).then_inc(sem("factor_copied"), 1)
            for q in range(2):
                ac.wait_ge(sem("hm_made"), q + 1)
                A(act[:, 4 * q:4 * q + 4, 0:T], qkvo[:, 4 * q:4 * q + 4, :], ACT.Copy).then_inc(sem("hm_hi"), 1)
            ac.wait_ge(sem("hm_split"), 2)

            into_conv = add_bias(conv_in, ("b_in_b", 0), "biased", lambda i: ACT.Identity)

            def conv_steps(j, ph, i, s):
                into_conv(j, ph, i, s)
                if j in (3, 4):
                    q = j - 3
                    ac.wait_ge(sem("conv_prod"), q + 1)
                    for m in range(GW):
                        f = 4 * q + m
                        last = A(conv_in[:, 8 + f, :], conv_pad[:, f, 2:2 + T], ACT.Copy, scale=col("conv_w", 16 + f))
                    last.then_inc(sem("conv_tap"), 1)
                elif j in (5, 6):
                    q = j - 5
                    ac.wait_ge(sem("conv_made"), q + 1)
                    A(act[:, 8 + 4 * q:12 + 4 * q, 0:T], conv_in[:, 8 + 4 * q:12 + 4 * q, :], ACT.Copy)\
                        .then_inc(sem("conv_hi"), 1)

            left = run("conv_in", into_conv, left, final=conv_steps)
            left = run("mix_gate", add_bias(mix_gate, ("b_in_b", 24), "mix_gate_ready", lambda i: ACT.Sigmoid), left)
            left = run("branch_m", low_only, left)

            def merged_high(j, ph, i, s):
                if j == 0:
                    low(ph, i, s)
                elif j == 1:
                    for q in (s,) if i == 0 else (2, 3) if s == 1 else ():
                        ac.wait_ge(sem("merged"), 1 + q + 1)
                        A(act[:, 4 * q:4 * q + 4, 0:T], mix_gate[:, 4 * q:4 * q + 4, :], ACT.Copy)\
                            .then_inc(sem("merged_hi"), 1)

            left = run("branch_c", merged_high, left)

            def residual(base, count=0, gain=None, gain_between=None):
                def step(j, ph, i, s):
                    g = 2 * i + s
                    if j == 0:
                        low(ph, i, s)
                    elif j == 1 and count:
                        ac.wait_ge(sem("h_added"), 1 + base + g + 1)
                        if gain_between is None:
                            square(count + g, g)
                        else:
                            square(count + 2 * g, g)
                            square(count + 2 * g, g, gain_between)
                        if gain is not None:
                            high(g, gain)
                return step

            left = run("out1", residual(0, 4, lambda t: dcol("norm_ffn_g", t)), left)

            def up(first, base, tiles=GW):
                def step(j, ph, i, s):
                    b = base + i
                    if j == 0:
                        low(ph, i, s, tiles)
                    elif j == 1:
                        scaled(ph, i, s)
                        for m in range(tiles):
                            t = s * FF_TILES + first + GW * i + m
                            last = A(up_conv[s][:, m, :], up_pad[s][:, m, 2:2 + T], ACT.Identity,
                                     bias=dcol("ffn_conv_b", t), scale=dcol("ffn_w2", t))
                        last.then_inc(sem("ff_tap"), 1)
                    elif j == 3 and s == 0:
                        ac.wait_ge(sem("ff_conv"), 2 * b + 1)
                        A(ysum[:, 0:tiles, :], up_conv[0][:, 0:tiles, :], ACT.Sigmoid).then_inc(sem("ff_sigmoid"), 1)
                    elif j == 4 and s == 1:
                        ac.wait_ge(sem("ff_made"), b + 1)
                        A(act[:, ds(first % 16 + GW * i, tiles), 0:T], made[:, 0:tiles, :], ACT.Copy)\
                            .then_inc(sem("ff_hi"), 1)
                return step

            left = run("up_0", up(0, 0), left, first=at_norm(1))
            left = run("down_0", low_only, left)
            left = run("up_1", up(16, 4), left)
            left = run("down_1", low_only, left)
            left = run("up_2", up(32, 8), left)
            left = run("up_3", up(40, 10, 3), left)
            left = run("down_2", residual(12, 8, lambda t: gain2[:, ds(t, 1)], lambda t: dcol("norm_out_g", t)), left)

            def both_roots(x):
                if x == MIDDLE + 1:
                    ac.wait_ge(sem("norm_total"), 3)
                    A(r1, psum[:, 4, 0:T], ACT.Sqrt, bias=eps[:, 0:1], scale=1.0 / D).then_inc(sem("norm_root"), 1)
                elif x == MIDDLE + 2:
                    ac.wait_ge(sem("second_sum_used"), 1)
                    A(r2, r2, ACT.Sqrt, bias=eps[:, 0:1], scale=1.0 / D).then_inc(sem("norm_root"), 1)

            def xc_high(q):
                ac.wait_ge(sem("xc_made"), 4 * q + 4)
                if q >= 2:
                    ac.wait_ge(half_used, 1 + 2 * PH["lru_gates"].c0 + 2 * (q - 2) + 2)
                A(xc_parts[q % 2][:, :, 0:TM], xc[:, 4 * q:4 * q + 4, :], ACT.Copy).then_inc(sem("xc_hi"), 1)

            def lru_conv(j, ph, i, s):
                if j in (1, 2, 3, 4):
                    if j == 1:
                        ac.wait_ge(psum_freed, PH["pool_in"].g0 + 2)
                    for m in range(GW):
                        f = 4 * (j - 1) + m
                        last = A(xc[:, f, :], lru_pad[:, f, 3:3 + TM], ACT.Identity,
                                 bias=col("conv_b_2", f), scale=col("conv_w_2", 3 * NT + f))
                    last.then_inc(sem("lru_tap"), 1)
                elif j in (5, 6):
                    xc_high(j - 5)

            left = run("lru_in", nothing, left, first=both_roots, final=lru_conv)
            left = run("pool_in", nothing, left)

            ph = PH["lru_gates"]
            for q in range(4):
                for s in range(2):
                    for k in range(HB(ph) // 2):
                        split(ph, q, AHEAD + s + k)
                for s, (dst, bias) in enumerate(((z_q, "gate_a_b_2"), (i_q, "gate_x_b_2"))):
                    ac.wait_ge(half_used, 1 + 2 * ph.c0 + 2 * q + s + 1)
                    if q:
                        ac.wait_ge(sem("lru_scanned"), q)
                    for m in range(GW):
                        last = A(dst[:, m, :], psum[:, 4 * s + m, 0:TM], ACT.Sigmoid, bias=col(bias, 4 * q + m))
                    last.then_inc(sem("gate_sigmoid"), 1)
                ac.wait_ge(sem("gate_sigmoid"), 2 * q + 2)
                for m in range(GW):
                    A(a_q[:, m, :], z_q[:, m, :], ACT.Exp, scale=sp8[:, 4 * q + m:4 * q + m + 1])
                    last = A(w_q[:, m, :], z_q[:, m, :], ACT.Tanh, scale=sp8[:, 4 * q + m:4 * q + m + 1])
                last.then_inc(sem("a_made"), 1)
                ac.wait_ge(sem("a_made"), q + 1)
                A(z_q, a_q, ACT.Square).then_inc(sem("a_squared"), 1)
                ac.wait_ge(sem("one_minus_a2"), q + 1)
                A(w_q, w_q, ACT.Sqrt, scale=-1.0, bias=tiny[:, 0:1]).then_inc(sem("mult_made"), 1)
                if q + 2 < 4:
                    xc_high(q + 2)

            def pool_high(x):
                if x in (2, 5, 9, 12):
                    g = (2, 5, 9, 12).index(x)
                    ac.wait_ge(sem("pool_diff"), g + 1)
                    A(act[:, 4 * g:4 * g + 4, 0:T], pool_v[:, 4 * g:4 * g + 4, META:TM], ACT.Copy).then_inc(sem("pool_hi"), 1)

            def gelu(j, ph, i, s):
                g = 2 * i + s
                if j == 0:
                    low(ph, i, s)
                elif j == 1:
                    scaled(ph, i, s)
                    A(ms, my, ACT.Square).then_inc(sem("gelu_square"), 1)
                elif j == 3:
                    ac.wait_ge(sem("gelu_inner"), 2 * g + 2)
                    A(ms, ms, ACT.Sigmoid, scale=1.5957691216057308).then_inc(sem("gelu_sigmoid"), 1)

            left = run("gelu", gelu, left, first=pool_high)
            left = run("pool_mix", low_only, left)

            def pool_gate(j, ph, i, s):
                if j == 0:
                    low(ph, i, s)
                elif j == 1:
                    scaled(ph, i, s)
                    A(ms, my, ACT.Sigmoid).then_inc(sem("gate_ready"), 1)

            def lru_gate(j, ph, i, s):
                g = 2 * i + s
                pool_gate(j, ph, i, s)
                if j == 3:
                    ac.wait_ge(sem("merged2"), g + 1)
                    A(act[:, ds(GW * g, GW), 0:T], pool_v[:, ds(GW * g, GW), META:TM], ACT.Copy)\
                        .then_inc(sem("merged2_hi"), 1)

            left = run("pool_gate", pool_gate, left)
            left = run("lru_gate", lru_gate, left)
            left = run("out2", residual(16, 16, lambda t: dcol("norm2_g_2", t)), left)

            def mlp(base):
                def step(j, ph, i, s):
                    g = 2 * i + s
                    if j == 0:
                        low(ph, i, s)
                    elif j == 1:
                        ac.wait_ge(sem("mlp_made"), base + g + 1)
                        A(act[:, ds(GW * g, GW), 0:T], made, ACT.Copy).then_inc(sem("mlp_hi"), 1)
                return step

            for q in range(4):
                left = run(f"mlp1_{q}", mlp(4 * q), left, first=at_norm(3) if q == 0 else None)
                left = run(f"mlp2_{q}", residual(32, 20) if q == 3 else low_only, left)
            left = finish(left)
            ac.wait_ge(sem("norm_total"), 5)
            A(rms_out[:, :], psum[:, 7, 0:2], ACT.Sqrt, bias=eps[:, 0:1], scale=1.0 / D).then_inc(sem("norm_root"), 1)
            ac.wait_ge(sem("rms_ready"), 1)
            for t in range(2):
                for q in (0, 2):
                    ac.wait_ge(sem("out_turned"), 2 * q + t + 1)
                    A(out_nat[:, t, q * 512:(q + 1) * 512], psum[:, 4 * t + q, :], ACT.Copy, scale=rms_out[:, t:t + 1])\
                        .then_inc(sem("out_copied_even"), 1)

        @block.vector
        def _(ve):
            V = nc.vector
            for name in STARTS_AT_ONE:
                ve.sem_inc(sem(name), 1)
            chain = [0]

            def link(ins):
                chain[0] += 1
                ins.then_inc(sem("vector_chain"), 1)
                ve.wait_ge(sem("vector_chain"), chain[0])

            def split(ph, i, loc):
                n = half_number(ph, i, loc)
                ve.wait_ge(hi_ready, 2 * ph.c0 + HB(ph) * i + loc + 1)
                V.tensor_tensor(wlo[:, n % SLOTS, :], raw[:, n // 2 % RAW, n % 2 * HALF:(n % 2 + 1) * HALF],
                                whi[:, n % SLOTS, :].bitcast(F32), ALU.subtract).then_inc(lo_ready, 1)

            def total(ph, i, s, dst, tiles=GW, unused=None):
                if unused is not None:
                    ve.wait_ge(*unused)
                ve.wait_ge(low_copied, ph.lc0 + 2 * i + s + 1)
                V.tensor_tensor(dst, psum[:, 4 * s:4 * s + tiles, 0:T], lowc[:, 0:tiles, :], ALU.add)\
                    .then_inc(psum_freed, 1)

            def totalled(ph, i, s):
                ve.wait_ge(psum_freed, ph.g0 + 2 * i + s + 3)

            def scaled_total(ph, i, s, dst, tiles=GW, unused=None):
                total(ph, i, s, dst, tiles, unused)
                totalled(ph, i, s)
                ve.wait_ge(sem("scale_ready"), ph.scale)
                V.tensor_tensor(dst, dst, over_tiles(stream_scale, tiles), ALU.mult).then_inc(sem("scaled"), 1)

            def scaled(ph, i, s):
                ve.wait_ge(sem("scaled"), ph.sc0 + 2 * i + s + 1)

            def run(name, step, left, first=None, final=None):
                return stream(ve, PH[name], split, step, left, first, final)

            def low_of(dst, src, high, done):
                V.tensor_tensor(dst, src, high.bitcast(F32), ALU.subtract).then_inc(done, 1)

            def sum_squares(count, g, src, dst):
                ve.wait_ge(sem("squared"), count + 1)
                V.tensor_reduce(dst[:, ds(g, 1), :].rearrange("p o t -> p (o t)"), src.rearrange("p k t -> p t k"),
                                AX.X, ALU.add).then_inc(sem("squares_summed"), 1)

            def low_operand(n, g, gain, wide=False):
                ve.wait_ge(sem("operand_hi"), 4 * n + g + 1)
                for again in range(2 if wide else 1):
                    for m in range(GW):
                        t = GW * g + m
                        dst = lo2[:, ds(t, 1), META:TM] if again else hn[:, ds(t, 1), META + T:META + 2 * T]
                        last = V.scalar_tensor_tensor(dst, h[:, ds(t, 1), :], gain(t),
                                                      hn[:, ds(t, 1), META:META + T].bitcast(F32),
                                                      ALU.mult, ALU.subtract)
                    last.then_inc(sem("lo2_made" if again else "operand_split"), 1)

            def scale_from_root(count):
                ve.wait_ge(sem("norm_root"), count)
                V.reciprocal(stream_scale, stream_scale).then_inc(sem("scale_ready"), 1)

            def copy_x(b):
                ve.wait_ge(sem("x_turned"), b + 1)
                V.tensor_copy(h[:, 2 * b:2 * b + 2, :], psum[:, b, :].rearrange("p (f t) -> p f t", t=T))\
                    .then_inc(sem("x_copied"), 1)

            for b in range(4):
                copy_x(b)
            ve.wait_ge(sem("cols_turned"), 1)
            for s, rws in enumerate(STAGES):
                nr = sum(n for _, n in rws)
                last = V.tensor_copy(cols[:, s * P:s * P + nr], psum[:, 4 + s // 4, (s % 4) * P:(s % 4) * P + nr])
                if s in (3, 5):
                    last.then_inc(sem("cols_copied"), 1)
            for q in range(4):
                if q >= 2:
                    copy_x(2 * q)
                    copy_x(2 * q + 1)
                ve.wait_ge(sem("x_copied"), 2 * q + 2)
                if q in (1, 3):
                    ve.sem_inc(psum_freed, 1)
                low_operand(0, q, lambda t: col("norm_mix_g", t))
                if q < AHEAD:
                    split(PH["qkvo"], 0, q)
                sum_squares(q, q, squares, part)
            ve.wait_ge(sem("gates_loaded"), 16)
            g0 = COLUMN["norm_mix_g"][0]
            V.tensor_tensor(wif, wif, cols[:, g0:g0 + NT].unsqueeze(2).to_broadcast([P, NT, 8]), ALU.mult)\
                .then_inc(sem("gates_scaled"), 1)
            ve.wait_ge(sem("meta_root"), 1)
            link(V.reciprocal(meta_ss[:, 1:2], meta_ss[:, 1:2]))
            V.tensor_scalar(meta_nat, meta_nat, meta_ss[:, 1:2], None, ALU.mult).then_inc(sem("meta_normed"), 1)
            c_out, c_in = COLUMN["norm_out_g"][0], COLUMN["norm1_g_2"][0]
            V.tensor_tensor(gain2[:, :], cols[:, c_out:c_out + NT], cols[:, c_in:c_in + NT], ALU.mult)\
                .then_inc(sem("gain2_made"), 1)

            def setup_sums(x):
                if x == MIDDLE + 1:
                    scale_from_root(1)
                    ve.wait_ge(sem("meta_turned"), 1)
                    g1 = COLUMN["norm1_g_2"][0]
                    meta_f = view(misc, 0, NT, META)
                    link(V.tensor_tensor(meta_f, psum[:, 6, 0:NT * META].rearrange("p (f t) -> p f t", t=META),
                                         cols[:, g1:g1 + NT].unsqueeze(2).to_broadcast([P, NT, META]), ALU.mult))
                    link(V.tensor_copy(hn[:, :, 0:META], meta_f))
                    link(V.tensor_tensor(meta_lo[:, :, :], meta_f, hn[:, :, 0:META].bitcast(F32), ALU.subtract))
                    ve.wait_ge(sem("gate_b_loaded"), 16)
                    ve.wait_ge(sem("if_made"), 1)
                    ve.wait_ge(sem("scale_ready"), 1)
                    link(V.tensor_tensor(logits, psum[0:8, 7, 0:T], stream_scale[0:8, :], ALU.mult))
                    V.tensor_scalar(logits, logits, gate_b[:, 0:1], None, ALU.add).then_inc(sem("logits_made"), 1)
                elif x == MIDDLE + 2:
                    ve.wait_ge(sem("lam_exp"), 1)
                    e, z, zz, s_ = lam
                    link(V.tensor_scalar(z, e, 2.0, None, ALU.add))
                    link(V.reciprocal(z, z))
                    link(V.tensor_tensor(z, z, e, ALU.mult))
                    link(V.tensor_tensor(zz, z, z, ALU.mult))
                    link(V.tensor_scalar(s_, zz, 1.0 / 19, 1.0 / 17, ALU.mult, ALU.add))
                    for k in range(7, -1, -1):
                        link(V.tensor_tensor(s_, s_, zz, ALU.mult))
                        link(V.tensor_scalar(s_, s_, 1.0 / (2 * k + 1), None, ALU.add))
                    link(V.scalar_tensor_tensor(s_, s_, 2.0, z, ALU.mult, ALU.mult))
                    c_lam = COLUMN["lru_lambda_2"][0]
                    link(V.tensor_scalar(z, cols[:, c_lam:c_lam + NT], -1.0, 0.0, ALU.mult, ALU.max))
                    link(V.tensor_tensor(s_, s_, z, ALU.add))
                    link(V.tensor_scalar(sp8[:, :], s_, -8.0, None, ALU.mult))

            def into(tiles, unused=None):
                def step(j, ph, i, s):
                    if j == 0:
                        scaled_total(ph, i, s, tiles[:, ds(GW * (2 * i + s), GW), :], unused=unused)
                return step

            left = (nothing, None, 0, 0)
            left = run("qkvo", into(qkvo), left, first=setup_sums)
            left = finish(left)

            ve.wait_ge(sem("f_moved"), 1)
            V.tensor_copy(row_c, psum[0:HEADS, 4, 0:T]).then_inc(sem("f_copied"), 1)
            ve.wait_ge(sem("f_copied"), 1)
            link(V.tensor_scalar(row_b, row_c, 0.0, None, ALU.min))
            ve.wait_ge(sem("f_step"), 3)
            link(V.tensor_tensor(row_b, row_b, row_a, ALU.subtract))
            link(V.tensor_tensor_scan(row_a, ones[0:HEADS, 0:T], row_b, 0.0, ALU.mult, ALU.add))
            link(V.tensor_tensor(row_c, logits[0:HEADS, :], row_a, ALU.subtract))
            link(V.tensor_tensor_scan(row_b, row_c, row_c, 0.0, ALU.max, ALU.max))
            V.tensor_tensor(row_guard, row_a, row_b, ALU.add).then_inc(sem("guard_sum"), 1)
            ve.sem_inc(sem("m_ready"), 1)
            for t in range(2):
                for j in range(2):
                    ve.wait_ge(sem("v_turned"), 2 * t + j + 1)
                    V.tensor_copy(v_tok[:, t, j * 512:(j + 1) * 512], psum[:, 2 * t + j, :]).then_inc(sem("v_copied"), 1)
            ve.wait_ge(sem("c_turned"), 1)
            V.tensor_copy(ccol[:, :, :], psum[:, 6, 0:2 * HEADS].rearrange("p (a b) -> p a b", b=HEADS))
            ve.wait_ge(sem("m_spread"), 1)
            spread = psum[:, 4:6, :].rearrange("p a (b t) -> p (a b) t", t=T)
            V.scalar_tensor_tensor(decay[:, :, 0:T], spread, -1.0,
                                   mask.unsqueeze(1).to_broadcast([P, HEADS, T]), ALU.mult, ALU.add)
            V.scalar_tensor_tensor(decay[:, :, T:T + P], spread[:, :, P:T], -1.0,
                                   mask[:, 0:P].unsqueeze(1).to_broadcast([P, HEADS, P]), ALU.mult, ALU.add)\
                .then_inc(sem("z_made"), 1)
            for hd in range(HEADS):
                ve.wait_ge(sem("decay_made"), hd + 1)
                ve.wait_ge(sem("scores_made"), hd + 1)
                V.scalar_tensor_tensor(scores[:, hd, :], psum[:, 6 + hd % 2, 0:T + P], DQK ** -0.5, decay[:, hd, :],
                                       ALU.mult, ALU.mult).then_inc(sem("st_made"), 1)
            ve.wait_ge(sem("den_abs"), 1)
            ve.wait_ge(sem("guard_ready"), 1)
            link(V.tensor_tensor(row_a, row_a, row_guard, ALU.max))
            link(V.reciprocal(row_a, row_a))
            link(V.tensor_tensor(row_b, row_a, row_a, ALU.mult))
            ve.wait_ge(sem("squares_used"), HEADS)
            V.tensor_tensor(row_b, row_b, psum[0:HEADS, 5, 0:T], ALU.mult).then_inc(sem("ms_made"), 1)
            ve.wait_ge(sem("ms_root"), 1)
            link(V.reciprocal(row_b, row_b))
            V.tensor_tensor(row_a, row_a, row_b, ALU.mult).then_inc(sem("factor_made"), 1)
            ve.wait_ge(sem("factor_copied"), 1)
            ve.wait_ge(sem("biased"), 6)
            for f in range(8):
                V.scalar_tensor_tensor(qkvo[:, f, :], psum[:, f // 2, f % 2 * T:(f % 2 + 1) * T],
                                       col("mlstm_head_g", f), factor[:, f // 2, :], ALU.mult, ALU.mult)\
                    .then_inc(sem("hm_scaled"), 1)
            for q in range(2):
                ve.wait_ge(sem("hm_scaled"), 4 * q + 4)
                t = qkvo[:, 4 * q:4 * q + 4, :]
                V.tensor_tensor(t, t, qkvo[:, 16 + 4 * q:20 + 4 * q, :], ALU.mult).then_inc(sem("hm_made"), 1)
            for q in range(2):
                ve.wait_ge(sem("hm_hi"), q + 1)
                low_of(act[:, 4 * q:4 * q + 4, T:2 * T], qkvo[:, 4 * q:4 * q + 4, :], act[:, 4 * q:4 * q + 4, 0:T],
                       sem("hm_split"))

            ve.wait_ge(sem("hm_split"), 2)
            V.memset(conv_pad[:, :, 0:2], 0.0).then_inc(sem("conv_cleared"), 1)
            into_conv = into(conv_in)

            def conv_steps(j, ph, i, s):
                into_conv(j, ph, i, s)
                if j == 2:
                    ve.wait_ge(sem("biased"), 12)
                    ve.wait_ge(sem("conv_cleared"), 1)
                    for q in range(2):
                        V.tensor_tensor(conv_pad[:, 4 * q:4 * q + 4, 2:2 + T], conv_in[:, 8 + 4 * q:12 + 4 * q, :],
                                        conv_in[:, 16 + 4 * q:20 + 4 * q, :], ALU.mult).then_inc(sem("conv_prod"), 1)
                if j in (4, 5):
                    q = j - 4
                    ve.wait_ge(sem("conv_tap"), q + 1)
                    for k in (1, 0):
                        for m in range(GW):
                            f = 4 * q + m
                            last = V.scalar_tensor_tensor(conv_in[:, 8 + f, :], conv_pad[:, f, k:k + T],
                                                          col("conv_w", 8 * k + f), conv_in[:, 8 + f, :],
                                                          ALU.mult, ALU.add)
                        link(last)
                    t = conv_in[:, 8 + 4 * q:12 + 4 * q, :]
                    V.tensor_tensor(t, t, conv_in[:, 4 * q:4 * q + 4, :], ALU.mult).then_inc(sem("conv_made"), 1)
                if j in (6, 7):
                    q = j - 6
                    ve.wait_ge(sem("conv_hi"), q + 1)
                    low_of(act[:, 8 + 4 * q:12 + 4 * q, T:2 * T], conv_in[:, 8 + 4 * q:12 + 4 * q, :],
                           act[:, 8 + 4 * q:12 + 4 * q, 0:T], sem("conv_split"))

            left = run("conv_in", into_conv, left, final=conv_steps)
            left = run("mix_gate", into(mix_gate, (sem("conv_split"), 2)), left)

            def branch_m(j, ph, i, s):
                if j == 0:
                    g = 2 * i + s
                    total(ph, i, s, my, unused=(sem("mixed_m"), 1 + g))
                    totalled(ph, i, s)
                    ve.wait_ge(sem("mix_gate_ready"), 8)
                    t = mix_gate[:, ds(GW * g, GW), :]
                    V.tensor_tensor(t, t, my, ALU.mult).then_inc(sem("mixed_m"), 1)

            left = run("branch_m", branch_m, left)

            def branch_c(j, ph, i, s):
                g = 2 * i + s
                if j == 0:
                    ve.wait_ge(sem("mixed_m"), 1 + 4)
                    total(ph, i, s, my, unused=(sem("merged"), 1 + g))
                    totalled(ph, i, s)
                    V.tensor_tensor(ms, mix_gate[:, ds(GW * g + NT, GW), :], my, ALU.mult).then_inc(sem("mixed_c"), 1)
                    ve.wait_ge(sem("mixed_c"), g + 1)
                    t = mix_gate[:, ds(GW * g, GW), :]
                    V.tensor_tensor(t, t, ms, ALU.add).then_inc(sem("merged"), 1)
                elif j == 2:
                    for q in (s,) if i == 0 else (2, 3) if s == 1 else ():
                        ve.wait_ge(sem("merged_hi"), q + 1)
                        low_of(act[:, 4 * q:4 * q + 4, T:2 * T], mix_gate[:, 4 * q:4 * q + 4, :],
                               act[:, 4 * q:4 * q + 4, 0:T], sem("merged_split"))

            left = run("branch_c", branch_c, left)

            def residual(base, count=0, n=None, gain=None, double=False, final=False):
                def step(j, ph, i, s):
                    g = 2 * i + s
                    t = h[:, ds(GW * g, GW), :]
                    if j == 0:
                        total(ph, i, s, ysum, unused=(sem("h_added"), 1 + base + g))
                        totalled(ph, i, s)
                        V.tensor_tensor(t, t, ysum, ALU.add).then_inc(sem("h_added"), 1)
                    elif j == 2 and count:
                        if double:
                            sum_squares(count + 2 * g, g, squares, part)
                            sum_squares(count + 2 * g + 1, g, squares2, part2)
                        else:
                            sum_squares(count + g, g, squares, part)
                        if final:
                            for m in range(GW):
                                f = h[:, 4 * g + m, :]
                                last = V.tensor_scalar(f, f, col("final_g_2", 4 * g + m), None, ALU.mult)
                            last.then_inc(sem("final_made"), 1)
                        else:
                            low_operand(n, g, gain, double)
                return step

            left = run("out1", residual(0, 4, 1, lambda t: dcol("norm_ffn_g", t)), left)
            for s in range(2):
                V.memset(up_pad[s][:, :, 0:2], 0.0).then_inc(sem("up_cleared"), 1)
            ve.wait_ge(sem("up_cleared"), 2)
            V.tensor_copy(lo2[:, :, 0:META], meta_lo[:, :, :].bitcast(F32)).then_inc(sem("lo2_made"), 1)

            def up(first, base, tiles=GW):
                def step(j, ph, i, s):
                    b = base + i
                    if j == 0:
                        scaled_total(ph, i, s, up_pad[s][:, 0:tiles, 2:2 + T], tiles)
                    elif j == 2:
                        ve.wait_ge(sem("ff_tap"), 2 * b + s + 1)
                        for k in (1, 0):
                            for m in range(tiles):
                                t = s * FF_TILES + first + GW * i + m
                                last = V.scalar_tensor_tensor(up_conv[s][:, m, :], up_pad[s][:, m, k:k + T],
                                                              dcol(f"ffn_w{k}", t), up_conv[s][:, m, :],
                                                              ALU.mult, ALU.add)
                            if k:
                                last.then_inc(sem("ff_conv_step"), 1)
                                ve.wait_ge(sem("ff_conv_step"), 2 * b + s + 1)
                        last.then_inc(sem("ff_conv"), 1)
                    elif j == 3 and s == 1:
                        ve.wait_ge(sem("ff_conv"), 2 * b + 2)
                        ve.wait_ge(sem("ff_sigmoid"), b + 1)
                        V.tensor_tensor(ysum[:, 0:tiles, :], up_conv[0][:, 0:tiles, :], ysum[:, 0:tiles, :], ALU.mult)\
                            .then_inc(sem("ff_silu"), 1)
                        ve.wait_ge(sem("ff_silu"), b + 1)
                        ve.wait_ge(sem("ff_split"), 1 + b)
                        V.tensor_tensor(made[:, 0:tiles, :], ysum[:, 0:tiles, :], up_conv[1][:, 0:tiles, :], ALU.mult)\
                            .then_inc(sem("ff_made"), 1)
                    elif j == 5 and s == 1:
                        ve.wait_ge(sem("ff_hi"), b + 1)
                        dst = act[:, ds(first % 16 + GW * i, tiles), :]
                        low_of(dst[:, :, T:2 * T], made[:, 0:tiles, :], dst[:, :, 0:T], sem("ff_split"))
                return step

            left = run("up_0", up(0, 0), left, first=lambda x: scale_from_root(2) if x == MIDDLE + 1 else None)
            left = run("down_0", residual(4), left)
            left = run("up_1", up(16, 4), left)
            left = run("down_1", residual(8), left)
            left = run("up_2", up(32, 8), left)
            left = run("up_3", up(40, 10, 3), left)
            left = run("down_2", residual(12, 8, 2, lambda t: gain2[:, ds(t, 1)], double=True), left)

            def both_norms(x):
                if x == MIDDLE + 1:
                    ve.wait_ge(sem("norm_root"), 3)
                    link(V.reciprocal(r1, r1))
                    link(V.tensor_tensor(r2, r1, r1, ALU.mult))
                    V.tensor_tensor(r2, r2, psum[:, 4, T:2 * T], ALU.mult).then_inc(sem("second_sum_used"), 1)
                elif x == MIDDLE + 2:
                    ve.wait_ge(sem("norm_root"), 4)
                    link(V.reciprocal(r2, r2))
                    V.tensor_tensor(stream_scale, r1, r2, ALU.mult).then_inc(sem("scale_ready"), 1)
                elif 8 <= x < 12:
                    if x == 8:
                        ve.wait_ge(sem("operand_split"), 12)
                    for f in range(4 * (x - 8), 4 * (x - 8) + 4):
                        last = V.scalar_tensor_tensor(h[:, f, :], h[:, f, :], col("norm_out_g", f), r1, ALU.mult, ALU.mult)
                    last.then_inc(sem("block_out"), 1)

            def copy_wide(dst, unused=None):
                def step(j, ph, i, s):
                    if j == 0:
                        if unused:
                            ve.wait_ge(*unused)
                        ve.wait_ge(half_used, 1 + 2 * ph.c0 + HB(ph) * i + (s + 1) * (HB(ph) // 2))
                        ve.wait_ge(sem("scale_ready"), ph.scale)
                        V.tensor_tensor(dst(2 * i + s), psum[:, 4 * s:4 * s + 4, 0:TM], over_tiles(scale[:, :]), ALU.mult)\
                            .then_inc(psum_freed, 1)
                return step

            def xc_low(q):
                ve.wait_ge(sem("xc_hi"), q + 1)
                x = xc_parts[q % 2]
                low_of(x[:, :, TM:2 * TM], xc[:, 4 * q:4 * q + 4, :], x[:, :, 0:TM], sem("xc_split"))

            into_lru = copy_wide(lambda g: lru_pad[:, ds(GW * g, GW), 3:3 + TM])

            def lru_conv(j, ph, i, s):
                into_lru(j, ph, i, s)
                if j == 1:
                    totalled(ph, i, s)
                    ve.wait_ge(sem("block_out"), 4)
                    V.memset(lru_pad[:, :, 0:3], 0.0).then_inc(sem("lru_cleared"), 1)
                    ve.wait_ge(sem("lru_cleared"), 1)
                elif j in (2, 3, 4, 5):
                    q = j - 2
                    ve.wait_ge(sem("lru_tap"), q + 1)
                    for k in (2, 1, 0):
                        for m in range(GW):
                            f = 4 * q + m
                            last = V.scalar_tensor_tensor(xc[:, f, :], lru_pad[:, f, k:k + TM],
                                                          col("conv_w_2", NT * k + f), xc[:, f, :], ALU.mult, ALU.add)
                            if k == 0:
                                last.then_inc(sem("xc_made"), 1)
                        if k:
                            link(last)
                elif j in (6, 7):
                    xc_low(j - 6)

            left = run("lru_in", into_lru, left, first=both_norms, final=lru_conv)
            left = run("pool_in", copy_wide(lambda g: pool_v[:, ds(GW * g, GW), :], (sem("xc_made"), NT)), left)

            ph = PH["lru_gates"]
            ve.wait_ge(psum_freed, ph.g0 + 2)
            for q in range(4):
                for s in range(2):
                    for k in range(HB(ph) // 2):
                        split(ph, q, AHEAD + s + k)
                x = xc[:, 4 * q:4 * q + 4, :]
                ve.wait_ge(sem("gate_sigmoid"), 2 * q + 1)
                ve.sem_inc(psum_freed, 1)
                ve.wait_ge(sem("gate_sigmoid"), 2 * q + 2)
                V.tensor_tensor(x, x, i_q, ALU.mult).then_inc(psum_freed, 1)
                totalled(ph, q, 1)
                ve.wait_ge(sem("a_squared"), q + 1)
                V.scalar_tensor_tensor(w_q, z_q, 1.0, w_q, ALU.add, ALU.mult).then_inc(sem("one_minus_a2"), 1)
                ve.wait_ge(sem("mult_made"), q + 1)
                link(V.tensor_tensor(x, x, w_q, ALU.mult))
                for m in range(GW):
                    t = xc[:, 4 * q + m, :]
                    last = V.tensor_tensor_scan(t, a_q[:, m, :], t, 0.0, ALU.mult, ALU.add)
                last.then_inc(sem("lru_scanned"), 1)
                if q + 2 < 4:
                    xc_low(q + 2)

            def pooling(x):
                if x in (1, 4, 8, 11):
                    g = (1, 4, 8, 11).index(x)
                    if g == 0:
                        ve.wait_ge(sem("lru_scanned"), 4)
                    v = pool_v[:, 4 * g:4 * g + 4, :]
                    src, w = v, 1
                    for level in range(g + 1):
                        dst = (a_q, w_q)[level % 2]
                        link(V.tensor_tensor(dst[:, :, 2 * w - 1:TM], src[:, :, 2 * w - 1:TM],
                                             src[:, :, w - 1:TM - w], ALU.add))
                        src, w = dst, 2 * w
                    V.scalar_tensor_tensor(v[:, :, META:TM], src[:, :, META:TM], 1.0 / w, v[:, :, META:TM],
                                           ALU.mult, ALU.subtract).then_inc(sem("pool_diff"), 1)
                elif x in (3, 6, 10, 13):
                    g = (3, 6, 10, 13).index(x)
                    ve.wait_ge(sem("pool_hi"), g + 1)
                    low_of(act[:, 4 * g:4 * g + 4, T:2 * T], pool_v[:, 4 * g:4 * g + 4, META:TM],
                           act[:, 4 * g:4 * g + 4, 0:T], sem("pool_split"))

            def gelu(j, ph, i, s):
                g = 2 * i + s
                if j == 0:
                    scaled_total(ph, i, s, my, unused=(sem("lru_out"), 1 + g))
                elif j == 2:
                    ve.wait_ge(sem("gelu_square"), g + 1)
                    V.tensor_scalar(ms, ms, 0.044715, 1.0, ALU.mult, ALU.add).then_inc(sem("gelu_inner"), 1)
                    ve.wait_ge(sem("gelu_inner"), 2 * g + 1)
                    V.tensor_tensor(ms, ms, my, ALU.mult).then_inc(sem("gelu_inner"), 1)
                elif j == 4:
                    ve.wait_ge(sem("gelu_sigmoid"), g + 1)
                    V.tensor_tensor(ms, ms, my, ALU.mult).then_inc(sem("gelu_made"), 1)
                    ve.wait_ge(sem("gelu_made"), g + 1)
                    t = xc[:, ds(GW * g, GW), META:TM]
                    V.tensor_tensor(t, t, ms, ALU.mult).then_inc(sem("lru_out"), 1)

            left = run("gelu", gelu, left, first=pooling)

            def pool_mix(j, ph, i, s):
                if j == 0:
                    g = 2 * i + s
                    ve.wait_ge(sem("lru_out"), 1 + 4)
                    total(ph, i, s, my, unused=(sem("pool_out"), g))
                    totalled(ph, i, s)
                    for m in range(GW):
                        last = V.tensor_scalar(pool_v[:, 4 * g + m, META:TM], my[:, m, :], col("pool_scale_2", 4 * g + m),
                                               None, ALU.mult)
                    last.then_inc(sem("pool_out"), 1)

            left = run("pool_mix", pool_mix, left)

            def pool_gate(j, ph, i, s):
                g = 2 * i + s
                if j == 0:
                    scaled_total(ph, i, s, my, unused=(sem("pool_out"), 4))
                elif j == 2:
                    ve.wait_ge(sem("gate_ready"), g + 1)
                    t = pool_v[:, ds(GW * g, GW), META:TM]
                    V.tensor_tensor(t, t, ms, ALU.mult).then_inc(sem("pool_gated"), 1)

            left = run("pool_gate", pool_gate, left)

            def lru_gate(j, ph, i, s):
                g = 2 * i + s
                if j == 0:
                    scaled_total(ph, i, s, my)
                elif j == 2:
                    ve.wait_ge(sem("gate_ready"), 4 + g + 1)
                    V.tensor_tensor(mt, xc[:, ds(GW * g, GW), META:TM], ms, ALU.mult).then_inc(sem("lru_gated"), 1)
                    ve.wait_ge(sem("lru_gated"), g + 1)
                    ve.wait_ge(sem("pool_gated"), 4)
                    t = pool_v[:, ds(GW * g, GW), META:TM]
                    V.tensor_tensor(t, t, mt, ALU.add).then_inc(sem("merged2"), 1)
                elif j == 4:
                    ve.wait_ge(sem("merged2_hi"), g + 1)
                    dst = act[:, ds(GW * g, GW), :]
                    low_of(dst[:, :, T:2 * T], pool_v[:, ds(GW * g, GW), META:TM], dst[:, :, 0:T], sem("merged2_split"))

            left = run("lru_gate", lru_gate, left)
            left = run("out2", residual(16, 16, 3, lambda t: dcol("norm2_g_2", t)), left)

            def mlp(base):
                def step(j, ph, i, s):
                    g = 2 * i + s
                    if j == 0:
                        scaled_total(ph, i, s, ysum, unused=(sem("h_added"), 1 + 20 + base))
                        scaled(ph, i, s)
                        ve.wait_ge(sem("mlp_split"), 1 + base + g)
                        V.scalar_tensor_tensor(made, ysum, 0.0, ysum, ALU.max, ALU.mult).then_inc(sem("mlp_made"), 1)
                    elif j == 2:
                        ve.wait_ge(sem("mlp_hi"), base + g + 1)
                        dst = act[:, ds(GW * g, GW), :]
                        low_of(dst[:, :, T:2 * T], made, dst[:, :, 0:T], sem("mlp_split"))
                return step

            for q in range(4):
                left = run(f"mlp1_{q}", mlp(4 * q), left,
                           first=(lambda x: scale_from_root(5) if x == MIDDLE + 1 else None) if q == 0 else None)
                left = run(f"mlp2_{q}", residual(20 + 4 * q, *((20, None, None, False, True) if q == 3 else ())), left)
            left = finish(left)
            ve.wait_ge(sem("norm_root"), 6)
            V.reciprocal(rms_out[:, :], rms_out[:, :]).then_inc(sem("rms_ready"), 1)
            ve.wait_ge(sem("rms_ready"), 1)
            for t in range(2):
                for q in (1, 3):
                    ve.wait_ge(sem("out_turned"), 2 * q + t + 1)
                    V.tensor_scalar(out_nat[:, t, q * 512:(q + 1) * 512], psum[:, 4 * t + q, :], rms_out[:, t:t + 1],
                                    None, ALU.mult).then_inc(sem("out_copied_odd"), 1)


_INS = ["x", "norm_mix_g", "w_in", "b_in", "mlstm_head_g", "w_branch_m", "conv_w", "w_branch_c", "w_out",
        "norm_ffn_g", "w_up", "ffn_conv_w", "ffn_conv_b", "w_down", "norm_out_g", "meta_tokens_2",
        "norm1_g_2", "w_in_2", "pool_w_2", "pool_scale_2", "conv_w_2", "conv_b_2", "gate_a_w_2",
        "gate_a_b_2", "gate_x_w_2", "gate_x_b_2", "lru_lambda_2", "w_out_2", "norm2_g_2", "mlp_w1_2",
        "mlp_w2_2", "final_g_2"]


def kernel(**inputs):
    import numpy as np
    import concourse.bacc as bacc
    from concourse.bass_utils import run_bass_kernel_spmd

    nc = bacc.Bacc("TRN2", target_bir_lowering=False, num_devices=1)
    arrays, args = {}, {}
    for name in _INS:
        array = np.ascontiguousarray(inputs[name])
        arrays[f"in_{name}"] = array
        args[name] = nc.dram_tensor(f"in_{name}", array.shape, mybir.dt.from_np(array.dtype),
                                    kind="ExternalInput").ap()
    out = nc.dram_tensor("out", (1, T, D), F32, kind="ExternalOutput").ap()
    build(nc, args, out)
    result = run_bass_kernel_spmd(nc, [arrays], core_ids=[0])
    return result.results[0]["out"]
```
